# Optimizing a Trainium2 kernel written in Bass

```python
import jax
import jax.numpy as jnp
from jax import lax
import math
import jax, jax.numpy as jnp
import numpy as np

D_MODEL = 1024
BATCH = 1
SEQ = 512
DEPTH = 2

MEM_LEN = 256
N_MIXERS = 3
HEAD_DIM = 64
N_MIX_HEADS = 12
MIX_WIDTH = N_MIX_HEADS * HEAD_DIM
N_MEM_HEADS = 4
MEM_WIDTH = N_MEM_HEADS * HEAD_DIM
OUT_WIDTH = MIX_WIDTH + MEM_WIDTH
Q_BLOCK = 128
MLA_Q_RANK = 256
MLA_KV_RANK = 128
MLA_NOPE_DIM = 64
MLA_ROPE_DIM = 32
MLA_QK_DIM = MLA_NOPE_DIM + MLA_ROPE_DIM
MLA_V_DIM = 64
ROPE_THETA = 10000.0
MOBA_BLOCK = 256
MOBA_TOPK = 3
D_FF = 2816
CONV_WIDTH = 3
EPS = 1e-6
POS_OFFSET_MAX = 1024

FOX_IN = 3 * MIX_WIDTH + N_MIX_HEADS + MEM_WIDTH
MLA_IN = MLA_Q_RANK + MLA_KV_RANK + MLA_ROPE_DIM + MEM_WIDTH
MOBA_IN = 3 * MIX_WIDTH + MEM_WIDTH


def rmsnorm(x, g):
    xf = x.astype(jnp.float32)
    y = xf * lax.rsqrt(jnp.mean(xf * xf, axis=-1, keepdims=True) + EPS)
    return (y * g.astype(jnp.float32)).astype(x.dtype)

def alibi_slopes(n_heads):
    return 2.0 ** (-8.0 * jnp.arange(1, n_heads + 1, dtype=jnp.float32) / n_heads)

def rope(x, cos, sin):
    half = x.shape[-1] // 2
    x1, x2 = x[..., :half], x[..., half:]
    return jnp.concatenate([x1 * cos - x2 * sin, x1 * sin + x2 * cos], axis=-1)

def to_heads(t, n_heads):
    b, s, _ = t.shape
    return t.reshape(b, s, n_heads, -1).transpose(0, 2, 1, 3)

def from_heads(t):
    b, h, s, d = t.shape
    return t.transpose(0, 2, 1, 3).reshape(b, s, h * d)

def causal_block_attention(q, k, v, log_decay=None):
    b, h, s, dk = q.shape
    nq = s // Q_BLOCK
    q_chunks = q.reshape(b, h, nq, Q_BLOCK, dk).transpose(2, 0, 1, 3, 4)
    key_idx = jnp.arange(s)
    xs = [q_chunks, jnp.arange(nq)]
    if log_decay is not None:
        xs.append(log_decay.reshape(b, h, nq, Q_BLOCK).transpose(2, 0, 1, 3))

    def step(args):
        qc, i = args[0], args[1]
        logits = jnp.einsum('bhqd,bhkd->bhqk', qc, k).astype(jnp.float32)
        if log_decay is not None:
            logits = logits + args[2][..., None] - log_decay[:, :, None, :]
        q_idx = i * Q_BLOCK + jnp.arange(Q_BLOCK)
        logits = jnp.where(key_idx[None, :] <= q_idx[:, None], logits, -jnp.inf)
        p = jax.nn.softmax(logits, axis=-1).astype(v.dtype)
        return jnp.einsum('bhqk,bhkd->bhqd', p, v)

    out = lax.map(step, tuple(xs))
    return out.transpose(1, 2, 0, 3, 4).reshape(b, h, s, v.shape[-1])

def fox_mixer(p, b_f, q_gain, k_gain):
    q, k, v, f = jnp.split(p, [MIX_WIDTH, 2 * MIX_WIDTH, 3 * MIX_WIDTH], axis=-1)
    q = rmsnorm(to_heads(q, N_MIX_HEADS), q_gain) * HEAD_DIM ** -0.5
    k = rmsnorm(to_heads(k, N_MIX_HEADS), k_gain)
    log_f = jax.nn.log_sigmoid(f.astype(jnp.float32) + b_f.astype(jnp.float32))
    cum = lax.cumsum(log_f, axis=1).transpose(0, 2, 1)
    return from_heads(causal_block_attention(q, k, to_heads(v, N_MIX_HEADS), cum))

def mla_mixer(p, cos, sin, qa_norm, kva_norm, w_q_up, w_kv_up, q_gain, k_gain):
    b, s, _ = p.shape
    q_lat, kv_lat, k_r = jnp.split(p, [MLA_Q_RANK, MLA_Q_RANK + MLA_KV_RANK], axis=-1)
    q = (rmsnorm(q_lat, qa_norm) @ w_q_up).reshape(b, s, N_MIX_HEADS, MLA_QK_DIM)
    kv = (rmsnorm(kv_lat, kva_norm) @ w_kv_up).reshape(b, s, N_MIX_HEADS, MLA_NOPE_DIM + MLA_V_DIM)
    q = jnp.concatenate([q[..., :MLA_NOPE_DIM], rope(q[..., MLA_NOPE_DIM:], cos, sin)], axis=-1)
    k_rope = jnp.broadcast_to(rope(k_r[:, :, None, :], cos, sin), (b, s, N_MIX_HEADS, MLA_ROPE_DIM))
    k = jnp.concatenate([kv[..., :MLA_NOPE_DIM], k_rope], axis=-1)
    v = kv[..., MLA_NOPE_DIM:]
    q = rmsnorm(q, q_gain).transpose(0, 2, 1, 3) * MLA_QK_DIM ** -0.5
    k = rmsnorm(k, k_gain).transpose(0, 2, 1, 3)
    return from_heads(causal_block_attention(q, k, v.transpose(0, 2, 1, 3)))

def moba_attention(q, k, v, positions, slopes):
    b, h, s, d = q.shape
    nb = -(-s // MOBA_BLOCK)
    pad = nb * MOBA_BLOCK - s
    kb = jnp.pad(k, ((0, 0), (0, 0), (0, pad), (0, 0))).reshape(b, h, nb, MOBA_BLOCK, d)
    vb = jnp.pad(v, ((0, 0), (0, 0), (0, pad), (0, 0))).reshape(b, h, nb, MOBA_BLOCK, d)
    posb = jnp.pad(positions, ((0, 0), (0, pad))).reshape(b, nb, MOBA_BLOCK)
    n_sel = min(MOBA_TOPK, nb - 1)
    nq = s // Q_BLOCK

    def chunks(t):
        tail = t.shape[3:]
        t = t.reshape((b, h, nq, Q_BLOCK) + tail)
        perm = (0, 2, 1, 3) + tuple(range(4, t.ndim))
        return t.transpose(perm).reshape((b * nq, h, Q_BLOCK) + tail)

    xs = [chunks(q), positions.reshape(b * nq, Q_BLOCK),
          jnp.repeat(jnp.arange(b), nq), jnp.tile(jnp.arange(nq), b)]
    if n_sel > 0:
        k_mean = kb.mean(axis=3)
        gate = jnp.einsum('bhsd,bhnd->bhsn', q, k_mean).astype(jnp.float32)
        q_blk = jnp.arange(s) // MOBA_BLOCK
        gate = jnp.where(jnp.arange(nb)[None, :] < q_blk[:, None], gate, -jnp.inf)
        g_val, g_idx = lax.top_k(gate, n_sel)
        xs += [chunks(g_idx), chunks(jnp.isfinite(g_val))]

    def step(args):
        qc, pq, bi, ci = args[0], args[1], args[2], args[3]
        t_idx = ci * Q_BLOCK + jnp.arange(Q_BLOCK)
        own = (ci * Q_BLOCK) // MOBA_BLOCK
        kb_b, vb_b, posb_b = kb[bi], vb[bi], posb[bi]
        k_own = lax.dynamic_index_in_dim(kb_b, own, axis=1, keepdims=False)
        v_own = lax.dynamic_index_in_dim(vb_b, own, axis=1, keepdims=False)
        pos_own = lax.dynamic_index_in_dim(posb_b, own, axis=0, keepdims=False)
        dist_own = (pq[:, None] - pos_own[None, :]).astype(jnp.float32)
        s_own = (jnp.einsum('hqd,hjd->hqj', qc, k_own).astype(jnp.float32)
                 - slopes[:, None, None] * dist_own[None])
        own_idx = own * MOBA_BLOCK + jnp.arange(MOBA_BLOCK)
        s_own = jnp.where(own_idx[None, None, :] <= t_idx[None, :, None], s_own, -jnp.inf)
        if n_sel == 0:
            p_own = jax.nn.softmax(s_own, axis=-1).astype(v.dtype)
            return jnp.einsum('hqj,hjd->hqd', p_own, v_own)
        idx, ok = args[4], args[5]
        k_sel = jax.vmap(lambda blocks, i: blocks[i])(kb_b, idx)
        v_sel = jax.vmap(lambda blocks, i: blocks[i])(vb_b, idx)
        dist_sel = (pq[None, :, None, None] - posb_b[idx]).astype(jnp.float32)
        s_sel = (jnp.einsum('hqd,hqkjd->hqkj', qc, k_sel).astype(jnp.float32)
                 - slopes[:, None, None, None] * dist_sel)
        s_sel = jnp.where(ok[..., None], s_sel, -jnp.inf).reshape(h, Q_BLOCK, n_sel * MOBA_BLOCK)
        p = jax.nn.softmax(jnp.concatenate([s_sel, s_own], axis=-1), axis=-1).astype(v.dtype)
        p_sel = p[..., :n_sel * MOBA_BLOCK].reshape(h, Q_BLOCK, n_sel, MOBA_BLOCK)
        p_own = p[..., n_sel * MOBA_BLOCK:]
        return (jnp.einsum('hqkj,hqkjd->hqd', p_sel, v_sel)
                + jnp.einsum('hqj,hjd->hqd', p_own, v_own))

    out = lax.map(step, tuple(xs))
    return out.reshape(b, nq, h, Q_BLOCK, d).transpose(0, 2, 1, 3, 4).reshape(b, h, s, d)

def moba_mixer(p, positions, q_gain, k_gain):
    q, k, v = jnp.split(p, [MIX_WIDTH, 2 * MIX_WIDTH], axis=-1)
    q = rmsnorm(to_heads(q, N_MIX_HEADS), q_gain) * HEAD_DIM ** -0.5
    k = rmsnorm(to_heads(k, N_MIX_HEADS), k_gain)
    out = moba_attention(q, k, to_heads(v, N_MIX_HEADS), positions, alibi_slopes(N_MIX_HEADS))
    return from_heads(out)

def memory_cross(qm, k_mem, v_mem, q_gain, k_gain):
    b, s, _ = qm.shape
    q = rmsnorm(qm.reshape(b, s, N_MEM_HEADS, HEAD_DIM), q_gain) * HEAD_DIM ** -0.5
    k = rmsnorm(k_mem, k_gain)
    logits = jnp.einsum('bshd,bmhd->bhsm', q, k).astype(jnp.float32)
    p = jax.nn.softmax(logits, axis=-1).astype(v_mem.dtype)
    return jnp.einsum('bhsm,bmhd->bshd', p, v_mem).reshape(b, s, MEM_WIDTH)

def conv_ffn(h, w_up, conv_w, conv_b, w_down):
    u = h @ w_up
    c = u.shape[-1]
    u = lax.conv_general_dilated(u, conv_w[:, None, :].astype(u.dtype), window_strides=(1,),
                                 padding=[(CONV_WIDTH - 1, 0)],
                                 dimension_numbers=('NWC', 'WIO', 'NWC'),
                                 feature_group_count=c) + conv_b
    gate, val = jnp.split(u, 2, axis=-1)
    return (jax.nn.silu(gate) * val) @ w_down

def first_inputs(seed: int = 0) -> dict:
    key = jax.random.key(seed)
    ks = iter(jax.random.split(key, 32))
    f32 = jnp.float32

    def dense(shape):
        return jax.random.normal(next(ks), shape, f32) * shape[-2] ** -0.5

    def gain(shape):
        return 1.0 + 0.05 * jax.random.normal(next(ks), shape, f32)

    n_fox = len(range(0, DEPTH, N_MIXERS))
    n_mla = len(range(1, DEPTH, N_MIXERS))
    n_moba = len(range(2, DEPTH, N_MIXERS))
    x = jax.random.normal(next(ks), (BATCH, SEQ, D_MODEL), f32)
    mem = jax.random.normal(next(ks), (BATCH, MEM_LEN, D_MODEL), f32)
    positions = (jnp.arange(SEQ, dtype=jnp.int32)[None, :]
                 + jax.random.randint(next(ks), (BATCH, 1), 0, POS_OFFSET_MAX, dtype=jnp.int32))
    return {
        'x': x,
        'mem': mem,
        'positions': positions,
        'norm_mix': gain((DEPTH, D_MODEL)),
        'norm_ffn': gain((DEPTH, D_MODEL)),
        'w_out': dense((DEPTH, OUT_WIDTH, D_MODEL)),
        'mem_norm': gain((D_MODEL,)),
        'w_mem_kv': dense((D_MODEL, 2 * MEM_WIDTH)),
        'mem_q_gain': gain((DEPTH, HEAD_DIM)),
        'mem_k_gain': gain((DEPTH, HEAD_DIM)),
        'fox_w_in': dense((n_fox, D_MODEL, FOX_IN)),
        'fox_b_f': jax.random.uniform(next(ks), (n_fox, N_MIX_HEADS), f32, 1.0, 5.0),
        'fox_q_gain': gain((n_fox, HEAD_DIM)),
        'fox_k_gain': gain((n_fox, HEAD_DIM)),
        'mla_w_in': dense((n_mla, D_MODEL, MLA_IN)),
        'mla_qa_norm': gain((n_mla, MLA_Q_RANK)),
        'mla_kva_norm': gain((n_mla, MLA_KV_RANK)),
        'mla_w_q_up': dense((n_mla, MLA_Q_RANK, N_MIX_HEADS * MLA_QK_DIM)),
        'mla_w_kv_up': dense((n_mla, MLA_KV_RANK, N_MIX_HEADS * (MLA_NOPE_DIM + MLA_V_DIM))),
        'mla_q_gain': gain((n_mla, MLA_QK_DIM)),
        'mla_k_gain': gain((n_mla, MLA_QK_DIM)),
        'moba_w_in': dense((n_moba, D_MODEL, MOBA_IN)),
        'moba_q_gain': gain((n_moba, HEAD_DIM)),
        'moba_k_gain': gain((n_moba, HEAD_DIM)),
        'ffn_w_up': dense((DEPTH, D_MODEL, 2 * D_FF)),
        'ffn_conv_w': dense((DEPTH, CONV_WIDTH, 2 * D_FF)),
        'ffn_conv_b': 0.01 * jax.random.normal(next(ks), (DEPTH, 2 * D_FF), f32),
        'ffn_w_down': dense((DEPTH, D_FF, D_MODEL)),
    }

def first_block(x, mem, positions, norm_mix, norm_ffn, w_out, mem_norm, w_mem_kv, mem_q_gain,
              mem_k_gain, fox_w_in, fox_b_f, fox_q_gain, fox_k_gain, mla_w_in, mla_qa_norm,
              mla_kva_norm, mla_w_q_up, mla_w_kv_up, mla_q_gain, mla_k_gain, moba_w_in,
              moba_q_gain, moba_k_gain, ffn_w_up, ffn_conv_w, ffn_conv_b, ffn_w_down):
    b, m = mem.shape[0], mem.shape[1]
    mem_kv = rmsnorm(mem, mem_norm) @ w_mem_kv
    k_mem = mem_kv[..., :MEM_WIDTH].reshape(b, m, N_MEM_HEADS, HEAD_DIM)
    v_mem = mem_kv[..., MEM_WIDTH:].reshape(b, m, N_MEM_HEADS, HEAD_DIM)
    inv_freq = ROPE_THETA ** (-jnp.arange(0, MLA_ROPE_DIM, 2, dtype=jnp.float32) / MLA_ROPE_DIM)
    ang = positions.astype(jnp.float32)[..., None] * inv_freq
    cos = jnp.cos(ang)[:, :, None, :].astype(x.dtype)
    sin = jnp.sin(ang)[:, :, None, :].astype(x.dtype)

    for i in range(DEPTH):
        kind, j = i % N_MIXERS, i // N_MIXERS
        h = rmsnorm(x, norm_mix[i])
        if kind == 0:
            p = h @ fox_w_in[j]
            o_mix = fox_mixer(p[..., :-MEM_WIDTH], fox_b_f[j], fox_q_gain[j], fox_k_gain[j])
        elif kind == 1:
            p = h @ mla_w_in[j]
            o_mix = mla_mixer(p[..., :-MEM_WIDTH], cos, sin, mla_qa_norm[j], mla_kva_norm[j],
                              mla_w_q_up[j], mla_w_kv_up[j], mla_q_gain[j], mla_k_gain[j])
        else:
            p = h @ moba_w_in[j]
            o_mix = moba_mixer(p[..., :-MEM_WIDTH], positions, moba_q_gain[j], moba_k_gain[j])
        o_mem = memory_cross(p[..., -MEM_WIDTH:], k_mem, v_mem, mem_q_gain[i], mem_k_gain[i])
        x = x + jnp.concatenate([o_mix, o_mem], axis=-1) @ w_out[i]
        x = x + conv_ffn(rmsnorm(x, norm_ffn[i]), ffn_w_up[i], ffn_conv_w[i], ffn_conv_b[i],
                         ffn_w_down[i])
    return x


DEPTH_2 = 1

ATTN_WIDTH = D_MODEL // 2
N_Q_HEADS = ATTN_WIDTH // HEAD_DIM
N_KV_HEADS = N_Q_HEADS // 4
Q_PER_KV = N_Q_HEADS // N_KV_HEADS
WINDOW = 128
BLOCK = 128
CONV_CH = D_MODEL // 4
CONV_WIDTH_2 = 31
MEM_WIDTH_2 = D_MODEL // 4
N_MEM_HEADS_2 = MEM_WIDTH_2 // HEAD_DIM
MIX_WIDTH_2 = ATTN_WIDTH + CONV_CH + MEM_WIDTH_2
ROPE_THETA_2 = 500000.0
ROPE_DIM = HEAD_DIM // 4
D_FF_2 = 256 * math.ceil(8 * D_MODEL / 3 / 256)

Q_COLS = N_Q_HEADS * HEAD_DIM
KV_COLS = N_KV_HEADS * HEAD_DIM
GLU_COLS = 2 * CONV_CH
MQ_COLS = N_MEM_HEADS_2 * HEAD_DIM
IN_COLS = Q_COLS + 2 * KV_COLS + GLU_COLS + MQ_COLS
SPLITS = [Q_COLS, Q_COLS + KV_COLS, Q_COLS + 2 * KV_COLS, Q_COLS + 2 * KV_COLS + GLU_COLS]


def rms_norm(x, g):
    xf = x.astype(jnp.float32)
    y = xf * lax.rsqrt(jnp.mean(xf * xf, axis=-1, keepdims=True) + EPS)
    return (y * g.astype(jnp.float32)).astype(x.dtype)

def layer_norm(x, g, b):
    xf = x.astype(jnp.float32)
    mu = jnp.mean(xf, axis=-1, keepdims=True)
    var = jnp.mean(jnp.square(xf - mu), axis=-1, keepdims=True)
    y = (xf - mu) * lax.rsqrt(var + EPS)
    return (y * g.astype(jnp.float32) + b.astype(jnp.float32)).astype(x.dtype)

def swiglu(x, w_gate, w_up, w_down):
    return (jax.nn.silu(x @ w_gate) * (x @ w_up)) @ w_down

def rope_partial(x, positions):
    half = ROPE_DIM // 2
    inv_freq = ROPE_THETA_2 ** (-jnp.arange(half, dtype=jnp.float32) / half)
    ang = positions.astype(jnp.float32)[..., None] * inv_freq
    cos = jnp.cos(ang)[:, :, None, :]
    sin = jnp.sin(ang)[:, :, None, :]
    xr = x[..., :ROPE_DIM].astype(jnp.float32)
    x1, x2 = xr[..., :half], xr[..., half:]
    rot = jnp.concatenate([x1 * cos - x2 * sin, x2 * cos + x1 * sin], axis=-1).astype(x.dtype)
    return jnp.concatenate([rot, x[..., ROPE_DIM:]], axis=-1)

def sliding_window_attention(q, k, v, sinks):
    B, T = q.shape[0], q.shape[1]
    nb = T // BLOCK
    qb = q.reshape(B, nb, BLOCK, N_KV_HEADS, Q_PER_KV, HEAD_DIM)

    def with_prev(a):
        a = a.reshape(B, nb, BLOCK, N_KV_HEADS, HEAD_DIM)
        prev = jnp.pad(a, ((0, 0), (1, 0), (0, 0), (0, 0), (0, 0)))[:, :-1]
        return jnp.concatenate([prev, a], axis=2)

    kb, vb = with_prev(k), with_prev(v)
    s = jnp.einsum('bnqgrd,bnkgd->bngrqk', qb, kb).astype(jnp.float32) * (HEAD_DIM ** -0.5)
    qi = jnp.arange(BLOCK)[:, None] + BLOCK
    ki = jnp.arange(2 * BLOCK)[None, :]
    rel = qi - ki
    band = (rel >= 0) & (rel < WINDOW)
    blk = jnp.arange(nb)[:, None, None]
    valid = band[None] & ((blk > 0) | (ki >= BLOCK)[None])
    s = jnp.where(valid[None, :, None, None], s, -jnp.inf)
    sink = sinks.astype(jnp.float32).reshape(N_KV_HEADS, Q_PER_KV)[None, None, :, :, None, None]
    m = jnp.maximum(jnp.max(s, axis=-1, keepdims=True), sink)
    p = jnp.exp(s - m)
    denom = jnp.sum(p, axis=-1, keepdims=True) + jnp.exp(sink - m)
    w = (p / denom).astype(v.dtype)
    o = jnp.einsum('bngrqk,bnkgd->bnqgrd', w, vb)
    return o.reshape(B, T, N_Q_HEADS * HEAD_DIM)

def memory_cross_attention(q, k, v):
    B, T = q.shape[0], q.shape[1]
    s = jnp.einsum('bthd,bmhd->bhtm', q, k).astype(jnp.float32) * (HEAD_DIM ** -0.5)
    w = jax.nn.softmax(s, axis=-1).astype(v.dtype)
    o = jnp.einsum('bhtm,bmhd->bthd', w, v)
    return o.reshape(B, T, N_MEM_HEADS_2 * HEAD_DIM)

def conformer_conv(u, w_dw, b_dw, g_ln, b_ln):
    a, gate = jnp.split(u, 2, axis=-1)
    h = a * jax.nn.sigmoid(gate)
    h = lax.conv_general_dilated(
        h, w_dw[:, None, :].astype(h.dtype), window_strides=(1,),
        padding=((CONV_WIDTH_2 - 1, 0),), dimension_numbers=('NWC', 'WIO', 'NWC'),
        feature_group_count=CONV_CH) + b_dw
    return jax.nn.silu(layer_norm(h, g_ln, b_ln))

def second_inputs(seed: int = 0) -> dict:
    key = jax.random.key(seed)
    ks = jax.random.split(key, 32)
    f32 = jnp.float32

    def w(k, shape, fan_in):
        return jax.random.normal(k, shape, f32) * (fan_in ** -0.5)

    def gain(k, shape):
        return 1.0 + 0.05 * jax.random.normal(k, shape, f32)

    L = DEPTH_2
    start = jax.random.randint(ks[2], (BATCH, 1), 0, 1024, dtype=jnp.int32)
    positions = start + jnp.arange(SEQ, dtype=jnp.int32)[None, :]
    return {
        "x": jax.random.normal(ks[0], (BATCH, SEQ, D_MODEL), f32),
        "mem": jax.random.normal(ks[1], (BATCH, MEM_LEN, D_MODEL), f32),
        "positions": positions,
        "g_ffn1": gain(ks[3], (L, D_MODEL)),
        "w_ffn1_gate": w(ks[4], (L, D_MODEL, D_FF_2), D_MODEL),
        "w_ffn1_up": w(ks[5], (L, D_MODEL, D_FF_2), D_MODEL),
        "w_ffn1_down": w(ks[6], (L, D_FF_2, D_MODEL), D_FF_2),
        "g_mix": gain(ks[7], (L, D_MODEL)),
        "w_in": w(ks[8], (L, D_MODEL, IN_COLS), D_MODEL),
        "g_q": gain(ks[9], (L, HEAD_DIM)),
        "g_k": gain(ks[10], (L, HEAD_DIM)),
        "sinks": 0.5 * jax.random.normal(ks[11], (L, N_Q_HEADS), f32),
        "w_dw": w(ks[12], (L, CONV_WIDTH_2, CONV_CH), CONV_WIDTH_2),
        "b_dw": 0.02 * jax.random.normal(ks[13], (L, CONV_CH), f32),
        "g_conv_ln": gain(ks[14], (L, CONV_CH)),
        "b_conv_ln": 0.02 * jax.random.normal(ks[15], (L, CONV_CH), f32),
        "g_mem": gain(ks[16], (L, D_MODEL)),
        "w_mem_kv": w(ks[17], (L, D_MODEL, 2 * MQ_COLS), D_MODEL),
        "g_mq": gain(ks[18], (L, HEAD_DIM)),
        "g_mk": gain(ks[19], (L, HEAD_DIM)),
        "w_out": w(ks[20], (L, MIX_WIDTH_2, D_MODEL), MIX_WIDTH_2),
        "g_ffn2": gain(ks[21], (L, D_MODEL)),
        "w_ffn2_gate": w(ks[22], (L, D_MODEL, D_FF_2), D_MODEL),
        "w_ffn2_up": w(ks[23], (L, D_MODEL, D_FF_2), D_MODEL),
        "w_ffn2_down": w(ks[24], (L, D_FF_2, D_MODEL), D_FF_2),
    }

def second_block(x, mem, positions, g_ffn1, w_ffn1_gate, w_ffn1_up, w_ffn1_down,
              g_mix, w_in, g_q, g_k, sinks, w_dw, b_dw, g_conv_ln, b_conv_ln,
              g_mem, w_mem_kv, g_mq, g_mk, w_out,
              g_ffn2, w_ffn2_gate, w_ffn2_up, w_ffn2_down):
    B, T = x.shape[0], x.shape[1]
    M = mem.shape[1]
    for l in range(DEPTH_2):
        x = x + 0.5 * swiglu(rms_norm(x, g_ffn1[l]), w_ffn1_gate[l], w_ffn1_up[l], w_ffn1_down[l])

        h = rms_norm(x, g_mix[l])
        proj = h @ w_in[l]
        q, k, v, u, mq = jnp.split(proj, SPLITS, axis=-1)
        q = q.reshape(B, T, N_Q_HEADS, HEAD_DIM)
        k = k.reshape(B, T, N_KV_HEADS, HEAD_DIM)
        v = v.reshape(B, T, N_KV_HEADS, HEAD_DIM)
        q = rope_partial(rms_norm(q, g_q[l]), positions)
        k = rope_partial(rms_norm(k, g_k[l]), positions)
        y_attn = sliding_window_attention(q, k, v, sinks[l])

        y_conv = conformer_conv(u, w_dw[l], b_dw[l], g_conv_ln[l], b_conv_ln[l])

        mkv = rms_norm(mem, g_mem[l]) @ w_mem_kv[l]
        mk, mv = jnp.split(mkv, 2, axis=-1)
        mq = rms_norm(mq.reshape(B, T, N_MEM_HEADS_2, HEAD_DIM), g_mq[l])
        mk = rms_norm(mk.reshape(B, M, N_MEM_HEADS_2, HEAD_DIM), g_mk[l])
        mv = mv.reshape(B, M, N_MEM_HEADS_2, HEAD_DIM)
        y_mem = memory_cross_attention(mq, mk, mv)

        x = x + jnp.concatenate([y_attn, y_conv, y_mem], axis=-1) @ w_out[l]

        x = x + 0.5 * swiglu(rms_norm(x, g_ffn2[l]), w_ffn2_gate[l], w_ffn2_up[l], w_ffn2_down[l])
    return x


def setup_inputs(seed=0):
    out = dict(first_inputs(seed))
    for name, value in second_inputs(seed + 1).items():
        if name != "x":
            out[name + "_2"] = value
    return out


def reference(
    x, mem, positions, norm_mix, norm_ffn, w_out, mem_norm, w_mem_kv, mem_q_gain, mem_k_gain,
    fox_w_in, fox_b_f, fox_q_gain, fox_k_gain, mla_w_in, mla_qa_norm, mla_kva_norm, mla_w_q_up,
    mla_w_kv_up, mla_q_gain, mla_k_gain, moba_w_in, moba_q_gain, moba_k_gain, ffn_w_up,
    ffn_conv_w, ffn_conv_b, ffn_w_down, mem_2, positions_2, g_ffn1_2, w_ffn1_gate_2,
    w_ffn1_up_2, w_ffn1_down_2, g_mix_2, w_in_2, g_q_2, g_k_2, sinks_2, w_dw_2, b_dw_2,
    g_conv_ln_2, b_conv_ln_2, g_mem_2, w_mem_kv_2, g_mq_2, g_mk_2, w_out_2, g_ffn2_2,
    w_ffn2_gate_2, w_ffn2_up_2, w_ffn2_down_2,
):
    x = first_block(
        x, mem, positions, norm_mix, norm_ffn, w_out, mem_norm, w_mem_kv, mem_q_gain,
        mem_k_gain, fox_w_in, fox_b_f, fox_q_gain, fox_k_gain, mla_w_in, mla_qa_norm,
        mla_kva_norm, mla_w_q_up, mla_w_kv_up, mla_q_gain, mla_k_gain, moba_w_in, moba_q_gain,
        moba_k_gain, ffn_w_up, ffn_conv_w, ffn_conv_b, ffn_w_down,
    )
    return second_block(
        x, mem_2, positions_2, g_ffn1_2, w_ffn1_gate_2, w_ffn1_up_2, w_ffn1_down_2, g_mix_2,
        w_in_2, g_q_2, g_k_2, sinks_2, w_dw_2, b_dw_2, g_conv_ln_2, b_conv_ln_2, g_mem_2,
        w_mem_kv_2, g_mq_2, g_mk_2, w_out_2, g_ffn2_2, w_ffn2_gate_2, w_ffn2_up_2,
        w_ffn2_down_2,
    )


_drawn_inputs = setup_inputs


def setup_inputs(seed=0):
    import zlib

    import numpy as np

    out = dict(_drawn_inputs(seed))
    spreads = {}
    factors = {'mem_norm': 8.0,
     'mem_q_gain': 8.0,
     'mem_k_gain': 8.0,
     'fox_q_gain': 4.802,
     'fox_k_gain': 4.248,
     'mla_qa_norm': 8.0,
     'mla_kva_norm': 5.012,
     'mla_q_gain': 8.0,
     'mla_k_gain': 8.0,
     'ffn_conv_b': 5.217,
     'g_ffn1_2': 3.58,
     'g_mix_2': 3.976,
     'g_q_2': 8.0,
     'g_k_2': 8.0,
     'sinks_2': 200.0,
     'b_dw_2': 33.816,
     'g_conv_ln_2': 30.685,
     'b_conv_ln_2': 64.0,
     'g_mem_2': 8.0,
     'g_mq_2': 8.0,
     'g_mk_2': 8.0,
     'g_ffn2_2': 3.858}
    for name, (base, spread) in spreads.items():
        noise = np.random.default_rng([zlib.crc32(name.encode()), seed]).standard_normal(out[name].shape)
        drawn = base * np.exp(spread * noise) if base else spread * noise
        out[name] = jnp.asarray(drawn.astype(out[name].dtype))
    for name, factor in factors.items():
        out[name] = (out[name] * factor).astype(out[name].dtype)
    return out
```

```python
from contextlib import ExitStack

import numpy as np
from concourse import mybir

F32 = mybir.dt.float32
F32R = mybir.dt.float32r
BF16 = mybir.dt.bfloat16
I32 = mybir.dt.int32
ALU = mybir.AluOpType
ACT = mybir.ActivationFunctionType
AX = mybir.AxisListType.X

T = 512
MEM = 256
D = 1024
KC = D // 128
FF = 2816
FC = FF // 128
HALF = FC // 2
EPS = 1e-6
NEG = -1.0e30
UT = 4
NRAW = 6
NSPL = 5
AHEAD = 3
TABLES = "natural_log_exp_and_others"
PI = float(np.pi)
C1 = 6.28125
C2 = float(np.float32(int((2 * np.pi - C1) * 2 ** 20) / 2 ** 20))
C3 = float(2 * np.pi - C1 - C2)


def weight_plan():
    t = []

    def out(name, layer, col, rows=8, row0=0):
        for k in range(rows):
            t.append((name, layer, row0 + 128 * k, col))

    def ffn(gate, up, down, layer, off):
        for s in range(2):
            for p in range(HALF):
                c = 128 * (HALF * s + p)
                out(gate, layer, c)
                out(up, layer, off + c)
            for c in range(8):
                out(down, layer, 128 * c, HALF, 128 * HALF * s)

    for c in range(21):
        out("fox", 0, 128 * c)
    for name in ("w_mem_kv", "w_mem_kv_2"):
        for c in range(4):
            out(name, 0, 128 * c)
    for c in range(8):
        out("w_out", 0, 128 * c)
    ffn("ffn_w_up", "ffn_w_up", "ffn_w_down", 0, FF)
    for c in range(6):
        out("mla", 0, 128 * c)
    for c in range(9):
        out("mla_q", 0, 128 * c, 2)
    for c in range(12):
        out("mla_kv", 0, 128 * c, 1)
    for c in range(8):
        out("w_out", 1, 128 * c)
    ffn("ffn_w_up", "ffn_w_up", "ffn_w_down", 1, FF)
    ffn("w_ffn1_gate_2", "w_ffn1_up_2", "w_ffn1_down_2", 0, 0)
    for c in range(12):
        out("w_in_2", 0, 128 * c)
    for c in range(8):
        out("w_out_2", 0, 128 * c)
    ffn("w_ffn2_gate_2", "w_ffn2_up_2", "w_ffn2_down_2", 0, 0)
    return t


PARAMS = [("mix0", 8), ("mix1", 8), ("nf0", 8), ("nf1", 8), ("memn", 8), ("f1", 8), ("mix2", 8), ("memn2", 8),
          ("f2", 8), ("mq0", 1), ("mq1", 1), ("foxq", 1), ("gq2", 1), ("gmq2", 1), ("mlaq", 1),
          ("mk0", 1), ("mk1", 1), ("foxk", 1), ("gk2", 1), ("gmk2", 1), ("mlak", 1), ("qa", 2), ("kva", 1),
          ("bf", 1), ("cw0", 132), ("cb0", 44), ("cw1", 132), ("cb1", 44), ("dw", 62), ("db", 2), ("lg", 2),
          ("lb", 2), ("sink", 8), ("fr0", 1), ("fr1", 1)]


def param_plan():
    at, n = {}, 0
    for name, k in PARAMS:
        at[name] = n
        n += k
    return at, n


class Queue:

    def __init__(self, sem):
        self.sem, self.ops, self.n, self.seen = sem, [], 0, {}

    def __call__(self, fn, *after, signal=True):
        self.wait(*after)
        self.ops.append((fn, self.sem if signal else None))
        if signal:
            self.n += 1
        return (self.sem, self.n) if signal else None

    def wait(self, *after):
        for a in after:
            if isinstance(a, list):
                self.wait(*a)
            elif a is not None and self.seen.get(a[0], 0) < a[1]:
                self.seen[a[0]] = a[1]
                self.ops.append((None, a))

    def play(self, eng):
        for fn, what in self.ops:
            if fn is None:
                eng.wait_ge(*what)
            else:
                ins = fn(eng)
                if what is not None:
                    ins.then_inc(what, 1)


class Ring:

    def __init__(self, items):
        self.items, self.free, self.at = items, [[] for _ in items], -1

    def take(self):
        self.at = (self.at + 1) % len(self.items)
        return self.at, self.items[self.at], self.free[self.at]


def program(nc, io):
    with ExitStack() as ctx:
        def sb(name, shape, dt=F32):
            return ctx.enter_context(nc.sbuf_tensor(name, shape, dt))

        def sem(name):
            return ctx.enter_context(nc.semaphore(name))

        PA, NPAR = param_plan()
        plan = weight_plan()
        n_units = (len(plan) + UT - 1) // UT

        pe, dve, act, pool_q, sp = (Queue(sem(n)) for n in ("s_pe", "s_dve", "s_act", "s_pool", "s_sp"))
        s_raw = [sem(f"s_raw{i}") for i in range(NRAW)]

        def pool(fn, *after, signal=True):
            return pool_q(fn, (pool_q.sem, pool_q.n) if pool_q.n else None, *after, signal=signal)

        def dma(dst, src, s, count, *after):
            sp.wait(*after)
            sp.ops.append((lambda e: e.dma_start(dst, src).then_inc(s, 16), None))
            return (s, count)

        XT = sb("XT", [128, KC, T])
        HNh = sb("HNh", [128, KC, T], F32R)
        HNl = sb("HNl", [128, KC, T], F32R)
        RAW = [sb(f"RAW{i}", [128, 128 * UT]) for i in range(NRAW)]
        WH = [sb(f"WH{i}", [128, 128 * UT], F32R) for i in range(NSPL)]
        WL = [sb(f"WL{i}", [128, 128 * UT], F32R) for i in range(NSPL)]
        PAR = sb("PAR", [128, NPAR])
        CONST = sb("CONST", [128, 512])
        IDENT, ONES, PM, PB = (CONST[:, 128 * i:128 * i + 128] for i in range(4))
        CB = sb("CB", [128, 384], BF16)
        IDB, MCAUS, MPREV = (CB[:, 128 * i:128 * i + 128] for i in range(3))
        CR = sb("CR", [128, 640], F32R)
        ONESR, BLKR, IDENTR = (CR[:, 128 * i:128 * i + 128] for i in range(3))

        def to_row(h):
            return CR[:, 384 + 127 - h:384 + 255 - h]
        sq_parts = Ring([(sb(f"SQH{i}", [128, T], F32R), sb(f"SQL{i}", [128, T], F32R)) for i in range(2)])
        ACC = sb("ACC", [128, T])
        EPSC = sb("EPSC", [128, 2])
        early = ExitStack()
        MT0 = early.enter_context(nc.sbuf_tensor("MT0", [128, 8, MEM], F32))
        early.close()
        ROPE = sb("ROPE", [128, 4, T])
        KMEM = sb("KMEM", [128, 3, 2, MEM])
        VMEM = sb("VMEM", [128, 2, 2, MEM])
        STAT = sb("STAT", [128, 2, 4, 16])
        NSINK = sb("NSINK", [128, 8])
        rs = Ring([sb(f"RS{i}", [128, T]) for i in range(2)])
        sq = Ring([sb(f"SQ{i}", [128, T]) for i in range(2)])
        tmp = Ring([sb(f"TMP{i}", [128, T]) for i in range(3)])
        base = nc.sbuf_base
        mixer = ExitStack()

        def mb(name, shape, dt=F32, stack=mixer):
            return stack.enter_context(nc.sbuf_tensor(name, shape, dt))

        QA = mb("QA", [128, 12, T])
        KA = mb("KA", [128, 12, T])
        VA = mb("VA", [128, 4, 768])
        MQ = mb("MQ", [128, 2, T])
        early = ExitStack()
        MT1 = early.enter_context(nc.sbuf_tensor("MT1", [128, 8, MEM], F32))
        ACCM = early.enter_context(nc.sbuf_tensor("ACCM", [128, 2, MEM], F32))
        early.close()
        pp = Ring([mb(f"PP{i}", [128, T]) for i in range(3)])
        pt = Ring([mb(f"PT{i}", [128, T]) for i in range(2)])
        OT = mb("OT", [128, D])
        mixer.close()
        ffn_mem = ExitStack()
        Gh = mb("Gh", [128, HALF, T], F32R, ffn_mem)
        Gl = mb("Gl", [128, HALF, T], F32R, ffn_mem)
        cv = Ring([mb(f"CV{i}", [128, T], F32, ffn_mem) for i in range(4)])
        gf = Ring([mb(f"GF{i}", [128, T], F32, ffn_mem) for i in range(2)])
        ffn_mem.close()

        PS = [ctx.enter_context(nc.psum_tensor(f"PS{i}", [128, T], F32)) for i in range(8)]
        bank_free = [[] for _ in range(8)]

        def par(name, i=0, rows=slice(0, 128), n=1):
            a = PA[name] + i
            return PAR[rows, a:a + n]

        s_par, s_const, s_cb, s_pos, s_x, s_mem = (sem(n) for n in ("s_par", "s_const", "s_cb", "s_pos", "s_x", "s_mem"))
        s_cum, s_out, s_cr = sem("s_cum"), sem("s_out"), sem("s_cr")

        class Weights:
            def __init__(self):
                self.at = 0
                self.raw_free = {}
                self.used = {}
                self.loaded = -1
                self.ready = {}

            def load_to(self, u):
                while self.loaded < min(u, n_units - 1):
                    self.loaded += 1
                    v = self.loaded
                    dma(RAW[v % NRAW][:, :], io["w"][v], s_raw[v % NRAW], 16 * (v // NRAW + 1),
                        self.raw_free.get(v - NRAW))

            def prepare(self, u):
                if u >= n_units or u in self.ready:
                    return
                r, h, l = RAW[u % NRAW], WH[u % NSPL], WL[u % NSPL]
                landed = (s_raw[u % NRAW], 16 * (u // NRAW + 1))
                a = act(lambda e: e.activation(h[:, :], r[:, :], ACT.Copy), landed, self.used.get(u - NSPL))
                b = dve(lambda e: e.tensor_tensor(l[:, :], r[:, :], h[:, :], ALU.subtract), landed, a,
                        self.used.get(u - NSPL))
                self.raw_free[u] = [a, b]
                self.ready[u] = [a, b]
                self.load_to(u + NRAW)

            def tile(self, key):
                assert plan[self.at] == key, (plan[self.at], key)
                u, j = divmod(self.at, UT)
                if j == 0:
                    for v in range(u, u + AHEAD + 1):
                        self.prepare(v)
                self.at += 1
                last = j == UT - 1 or self.at == len(plan)
                c = slice(128 * j, 128 * j + 128)
                return WH[u % NSPL][:, c], WL[u % NSPL][:, c], self.ready[u], (u if last else None)

        W = Weights()

        tasks = []

        slow = []

        def tick():
            for some in (tasks, slow):
                for t in list(some):
                    try:
                        next(t)
                    except StopIteration:
                        some.remove(t)

        def start(t):
            tasks.append(t)

        def flush():
            while tasks:
                tick()

        dense_at = [0]

        def dense(name, layer, col, rhs, N=T, row0=0, banks=(0, 1, 2, 3, 4)):
            b = banks[dense_at[0] % len(banks)]
            dense_at[0] += 1
            pe.wait(bank_free[b])
            n = len(rhs)
            for k, (xh, xl, got) in enumerate(rhs):
                wh, wl, ready, last = W.tile((name, layer, row0 + 128 * k, col))
                out = PS[b][:, 0:N]
                pe(lambda e, o=out, a=wh, x=xh, k=k: e.matmul(o, a, x, start=(k == 0), stop=False),
                   ready, got, signal=False)
                pe(lambda e, o=out, a=wh, x=xl: e.matmul(o, a, x, start=False, stop=False), signal=False)
                t = pe(lambda e, o=out, a=wl, x=xh, k=k: e.matmul(o, a, x, start=False, stop=(k == n - 1)),
                       signal=(last is not None or k == n - 1))
                if last is not None:
                    W.used[last] = t
            return b, t

        def split(src, h, l, *after):
            a = act(lambda e: e.activation(h, src, ACT.Copy), *after)
            b = dve(lambda e: e.tensor_tensor(l, src, h, ALU.subtract), a, *after)
            return [a, b]

        def rsqrt(bank, rows, N, scale, done):
            j, R, free = rs.take()
            a = act(lambda e: e.activation(R[rows, 0:N], PS[bank][rows, 0:N], ACT.Ln, bias=EPSC[rows, 0:1],
                                           scale=scale), done, free, t_eps)
            bank_free[bank] = [a]
            a = act(lambda e: e.activation(R[rows, 0:N], R[rows, 0:N], ACT.Exp, scale=-0.5), a)
            return j, R, a

        aux = [0]

        def aux_bank():
            aux[0] += 1
            return 5 + aux[0] % 2

        class ColumnNorm:

            def __init__(self, X, gain, N=T, at=0, acc=None, hn_free=None):
                self.X, self.gain, self.N, self.at0, self.n = X, gain, N, at, 0
                self.acc, self.hn_free = (ACC[:, :] if acc is None else acc), hn_free
                self.out, self.fed, self.r = [], [], None

            def part(self, c, token, hn_free):
                N, o = self.N, self.at0
                h, l = HNh[:, c, o:o + N], HNl[:, c, o:o + N]
                a = act(lambda e: e.activation(h, self.X[:, c, 0:N], ACT.Copy, scale=par(self.gain, c)), token,
                        hn_free, t_par)
                b = dve(lambda e: e.scalar_tensor_tensor(l, self.X[:, c, 0:N], par(self.gain, c), h, ALU.mult,
                                                         ALU.subtract), a, token, hn_free, t_par)
                self.out.append((h, l, [a, b]))

            def feed(self, c, token):
                N = self.N
                if self.hn_free is not None:
                    self.part(c, token, self.hn_free)
                j, S, free = sq.take()
                a = act(lambda e: e.activation(S[:, 0:N], self.X[:, c, 0:N], ACT.Square), token, free)
                self.fed.append(token)
                if self.n == 0:
                    self.sum = dve(lambda e: e.tensor_copy(self.acc, S[:, 0:N]), a)
                else:
                    self.sum = dve(lambda e: e.tensor_tensor(self.acc, self.acc, S[:, 0:N], ALU.add), a, self.sum)
                sq.free[j] = [self.sum]
                self.n += 1

            def feed_all(self, token):
                for c in range(KC):
                    self.feed(c, token)

            def total(self):
                N = self.N
                p = pe(lambda e: e.matmul(PS[7][:, 0:N], ONES, self.acc, start=True, stop=True),
                       self.sum, t_const, bank_free[7])
                a = act(lambda e: e.activation(self.acc, PS[7][:, 0:N], ACT.Ln, bias=EPSC[:, 0:1], scale=1.0 / D),
                        p, t_eps)
                bank_free[7] = [a]
                self.r = act(lambda e: e.activation(self.acc, self.acc, ACT.Exp, scale=-0.5), a)

            def finish(self, hn_free):
                if not self.out:
                    for c in range(KC):
                        self.part(c, self.fed[c], hn_free)

            def normed(self, name, layer, col):
                b, p = dense(name, layer, col, self.out, self.N)
                if self.r is None:
                    self.total()
                out = PS[b][:, 0:self.N]
                return b, dve(lambda e: e.tensor_tensor(out, out, self.acc, ALU.mult), p, self.r), p

        def square_sums(S, r, N, ones, a):
            w, (SQH, SQL), free = sq_parts.take()
            t = split(S[r, 0:N], SQH[r, 0:N], SQL[r, 0:N], a, free)

            def sums(j, scale):
                b = aux_bank()
                pe(lambda e: e.matmul(PS[b][:, 0:N], ones[r, :], SQH[r, 0:N], start=True, stop=False), t, t_cr,
                   bank_free[b], signal=False)
                p = pe(lambda e: e.matmul(PS[b][:, 0:N], ones[r, :], SQL[r, 0:N], start=False, stop=True))
                sq_parts.free[w] = [p]
                i, R, free = rs.take()
                x = dve(lambda e: e.tensor_scalar(S[r, 0:N], PS[b][r, 0:N], scale, EPS, ALU.mult, ALU.add), p, t, a)
                bank_free[b] = [x]
                y = act(lambda e: e.activation(R[r, 0:N], S[r, 0:N], ACT.Ln), x, free)
                y = act(lambda e: e.activation(R[r, 0:N], R[r, 0:N], ACT.Exp, scale=-0.5), y)
                z = pool(lambda e: e.tensor_tensor(S[r, 0:N], S[r, 0:N], R[r, 0:N], ALU.mult), y)
                z = dve(lambda e: e.scalar_tensor_tensor(S[r, 0:N], S[r, 0:N], -0.5, R[r, 0:N], ALU.mult, ALU.mult), z)
                z = dve(lambda e: e.scalar_tensor_tensor(R[r, 0:N], S[r, 0:N], 1.5, R[r, 0:N], ALU.add, ALU.mult), z)
                sq.free[j] = [z]
                return i, R, z, x
            return sums

        def head_norm(bank, done, N, scale, outs, res):
            r = slice(0, 128)
            j, S, free = sq.take()
            a = act(lambda e: e.activation(S[:, 0:N], PS[bank][:, 0:N], ACT.Square), done, free)
            sums = square_sums(S, r, N, BLKR, a)
            yield
            i, R, y, a = sums(j, scale)
            got = []
            for rows, gain, dst in outs:
                got.append(dve(lambda e, r=rows, g=gain, d=dst: e.scalar_tensor_tensor(
                    d, PS[bank][r, 0:N], par(g, 0, r), R[r, 0:N], ALU.mult, ALU.mult), y, a, done, t_gain))
            rs.free[i] = got[-1:]
            bank_free[bank] = [a] + got[-1:]
            res.extend(got[-1:])

        def to_rows(bank, done, N, put, res):
            i, B, free = tmp.take()
            a = act(lambda e: e.activation(B[:, 0:N], PS[bank][:, 0:N], ACT.Copy), done, free)
            bank_free[bank] = [a]
            yield
            b = aux_bank()
            for k in range(N // 128):
                p = pe(lambda e, k=k: e.transpose(PS[b][:, 128 * k:128 * k + 128], B[:, 128 * k:128 * k + 128], IDENT),
                       a, t_const, bank_free[b] if k == 0 else [], signal=(k == N // 128 - 1))
            tmp.free[i] = [p]
            t = dve(lambda e: put(e, PS[b][:, 0:N].rearrange("p (k f) -> p k f", f=128)), p)
            bank_free[b] = [t]
            res.append(t)

        def rope(src, got, which, rot, adds, res):
            b = aux_bank()
            p = pe(lambda e: e.matmul(PS[b][:, :], rot, src, start=True, stop=True), got, t_const, bank_free[b])
            i, A, fa = tmp.take()
            k, B, fb = tmp.take()
            x = dve(lambda e: e.tensor_tensor(A[:, :], src, ROPE[:, 2 * which, :], ALU.mult), got, fa, t_rope)
            y = dve(lambda e: e.tensor_tensor(B[:, :], PS[b][:, :], ROPE[:, 2 * which + 1, :], ALU.mult), p, fb, t_rope)
            bank_free[b] = [y]
            for rows, dst in adds:
                z = dve(lambda e, r=rows, d=dst: e.tensor_tensor(d, A[r, :], B[r, :], ALU.add), x, y)
                res.append(z)
            tmp.free[i] = tmp.free[k] = [z]
            return p

        class Item:
            def __init__(self, q, k, masks, nk, vals, slot, got, sink=None):
                self.q, self.k, self.masks, self.nk, self.vals = q, k, masks, nk, vals
                self.slot, self.got, self.sink = slot, got, sink

        sring, tring = [0], [0]
        hn_used = [None]

        def attention(tiles, got_hn):
            state = {}
            flat = [(i, n, it) for i, items in enumerate(tiles) for n, it in enumerate(items)]
            stat = {}

            def score(i, n, it):
                b = sring[0] % 3
                sring[0] += 1
                pe.wait(bank_free[b], it.got, t_cb)
                p = pe(lambda e: e.matmul(PS[b][:, 0:it.nk], it.q, it.k, start=True, stop=not it.masks),
                       signal=not it.masks)
                for m, (c, mask) in enumerate(it.masks):
                    last = m == len(it.masks) - 1
                    p = pe(lambda e, c=c, mask=mask, last=last: e.matmul(PS[b][:, c:c + 128], IDB, mask,
                                                                         start=False, stop=last), signal=last)
                St = STAT[:, i % 2]
                s = it.slot
                m = dve(lambda e: e.tensor_reduce(St[:, 0, s:s + 1], PS[b][:, 0:it.nk], AX, ALU.max, negate=True),
                        p, stat.get(i - 2, []))
                if it.sink is not None:
                    m = dve(lambda e: e.tensor_tensor(St[:, 0, s:s + 1], St[:, 0, s:s + 1],
                                                      NSINK[:, it.sink:it.sink + 1], ALU.min), m, t_gain)
                j, P, free = pp.take()
                a = act(lambda e: e.activation(P[:, 0:it.nk], PS[b][:, 0:it.nk], ACT.Exp, bias=St[:, 0, s:s + 1],
                                               accum_out=St[:, 1, s:s + 1]), m, p, free, stat.get(i - 2, []))
                bank_free[b] = [a]
                return j, P, a

            def turn(i, n, it, j, P, a):
                b = 3 + tring[0] % 2
                tring[0] += 1
                pe.wait(bank_free[b], a)
                for k in range(it.nk // 128):
                    p = pe(lambda e, k=k: e.transpose(PS[b][:, 128 * k:128 * k + 128], P[:, 128 * k:128 * k + 128],
                                                      IDENT), signal=(k == it.nk // 128 - 1))
                pp.free[j] = [p]
                m, Q, free = pt.take()
                if tring[0] % 2:
                    t = dve(lambda e: e.tensor_copy(Q[:, 0:it.nk], PS[b][:, 0:it.nk]), p, free)
                else:
                    t = act(lambda e: e.activation(Q[:, 0:it.nk], PS[b][:, 0:it.nk], ACT.Copy), p, free)
                bank_free[b] = [t]
                return m, Q, t

            def values(i, n, it, m, Q, t):
                b, c = 6 + it.slot // 8, 64 * (it.slot % 8)
                first = it.slot in (0, 8)
                pe.wait(t, it.got, bank_free[b] if n == 0 or it.slot in (0, 8, 12) else [])
                nb = it.nk // 128
                for k in range(nb):
                    p = pe(lambda e, k=k: e.matmul(PS[b][:, c:c + 64], Q[:, 128 * k:128 * k + 128], it.vals[k],
                                                   start=(k == 0), stop=(k == nb - 1)), signal=(k == nb - 1))
                pt.free[m] = [p]
                return p

            def finish(i, p, a):
                St = STAT[:, i % 2]
                items = tiles[i]
                sinks = items[0].sink is not None
                used = sorted(it.slot for it in items)
                runs = [(lo, min(hi, lo + 8)) for lo in (0, 8) for hi in [lo + sum(1 for s in used if lo <= s < lo + 8)] if hi > lo]
                if sinks:
                    x = dve(lambda e: e.tensor_tensor(St[:, 2, 0:8], par("sink", 0, n=8), St[:, 0, 0:8], ALU.add), t_par, a)
                    x = act(lambda e: e.activation(St[:, 2, 0:8], St[:, 2, 0:8], ACT.Exp), x)
                    a = [a, dve(lambda e: e.tensor_tensor(St[:, 1, 0:8], St[:, 1, 0:8], St[:, 2, 0:8], ALU.add), x, a)]
                outs = []
                for lo, hi in runs:
                    r = dve(lambda e, lo=lo, hi=hi: e.reciprocal(St[:, 3, lo:hi], St[:, 1, lo:hi]), a)
                    b, w = 6 + lo // 8, hi - lo
                    free = state.get("ot", [])
                    t = dve(lambda e, b=b, w=w, lo=lo, hi=hi: e.tensor_tensor(
                        OT[:, 64 * lo:64 * hi].rearrange("p (h d) -> p h d", d=64),
                        PS[b][:, 0:64 * w].rearrange("p (h d) -> p h d", d=64),
                        St[:, 3, lo:hi].unsqueeze(2).broadcast_to([128, w, 64]), ALU.mult), r, p, free)
                    bank_free[b] = [t]
                    outs.append((lo, hi, t))
                stat[i] = [t]
                return outs

            def spread(i, outs):
                yield
                for lo, hi, t in outs:
                    nb = (hi - lo) // 2
                    for k0 in range(0, nb, 4):
                        m = min(4, nb - k0)
                        c0 = lo // 2 + k0
                        oc = chunk_of(c0)
                        for k in range(m):
                            c = 128 * (c0 + k)
                            p = pe(lambda e, k=k, c=c: e.transpose(PS[5][:, 128 * k:128 * k + 128], OT[:, c:c + 128], IDENT),
                                   t, bank_free[5] if k == 0 else [], signal=(k == m - 1))
                        src = PS[5][:, 0:128 * m].rearrange("p (k f) -> p k f", f=128)
                        dst = (slice(None), slice(oc, oc + m), slice(128 * i, 128 * i + 128))
                        bank_free[5] = split(src, HNh[dst], HNl[dst], p, got_hn)
                        result.extend(bank_free[5])
                state["ot"] = [p]

            result = []
            fill = {}
            n_items = len(flat)
            A, B = {}, {}
            for s in range(n_items + 3):
                if s < n_items:
                    A[s] = score(*flat[s])
                if 0 <= s - 2 < n_items:
                    B[s - 2] = turn(*flat[s - 2], *A[s - 2])
                if 0 <= s - 3 < n_items:
                    i, n, it = flat[s - 3]
                    p = values(i, n, it, *B[s - 3])
                    if n == len(tiles[i]) - 1:
                        start(spread(i, finish(i, p, A[s - 3][2])))
                tick()
            flush()
            return result

        chunk_map = [None]

        def chunk_of(c):
            return chunk_map[0](c)

        def project(name, layer, got, norm=None, hn=None):
            rhs = [(HNh[:, c, :], HNl[:, c, :], got) for c in range(KC)]
            for c in range(KC):
                b, p = dense(name, layer, 128 * c, rhs)
                t = dve(lambda e, b=b, c=c: e.tensor_tensor(XT[:, c, :], PS[b][:, :], XT[:, c, :], ALU.add), p)
                bank_free[b] = [t]
                norm.feed(c, t)
                tick()
            return p

        def ffn(gate, up, down, layer, off, last, conv, weight, norm):
            g_free = [None]
            for s in range(2):
                parts = [None] * HALF

                def conv_part(b, p, idx, lay, box):
                    k, B, free = cv.take()
                    w = lambda tap: par(f"cw{lay}", 3 * idx + tap)
                    a = act(lambda e: e.activation(B[:, :], PS[b][:, :], ACT.Identity, bias=par(f"cb{lay}", idx),
                                                   scale=w(2)), p, free, t_par)
                    a = dve(lambda e: e.scalar_tensor_tensor(B[:, 1:T], PS[b][:, 0:T - 1], w(1), B[:, 1:T],
                                                             ALU.mult, ALU.add), a, p)
                    a = dve(lambda e: e.scalar_tensor_tensor(B[:, 2:T], PS[b][:, 0:T - 2], w(0), B[:, 2:T],
                                                             ALU.mult, ALU.add), a)
                    bank_free[b] = [a]
                    box.append((k, B, a))

                for q in range(HALF):
                    c = HALF * s + q
                    if conv:
                        box = []
                        for idx in (c, FC + c):
                            b, p, hn_done = last.normed(gate, layer, 128 * idx)
                            conv_part(b, p, idx, layer, box)
                            tick()
                        (k0, A, ta), (k1, B, tb) = box
                        a = act(lambda e, A=A: e.activation(A[:, :], A[:, :], ACT.Silu), ta)
                        i, G, free = gf.take()
                        t = dve(lambda e, G=G, A=A, B=B: e.tensor_tensor(G[:, :], A[:, :], B[:, :], ALU.mult), a, tb, free)
                        cv.free[k0] = cv.free[k1] = [t]
                    else:
                        b, p, _ = last.normed(gate, layer, 128 * c)
                        k0, A, free = cv.take()
                        a = act(lambda e, A=A, b=b: e.activation(A[:, :], PS[b][:, :], ACT.Silu), p, free)
                        bank_free[b] = [a]
                        tick()
                        b, p, hn_done = last.normed(up, layer, 128 * c)
                        i, G, free = gf.take()
                        t = dve(lambda e, G=G, A=A, b=b: e.tensor_tensor(G[:, :], A[:, :], PS[b][:, :], ALU.mult),
                                a, p, free)
                        cv.free[k0] = [t]
                        bank_free[b] = [t]
                        tick()
                    h, l = Gh[:, q, :], Gl[:, q, :]
                    w = split(G[:, :], h, l, t, g_free[0])
                    gf.free[i] = w
                    parts[q] = (h, l, w)
                if s == 1 and norm is not None:
                    norm.hn_free = [hn_done]
                for c in range(KC):
                    b, p = dense(down, layer, 128 * c, parts, row0=128 * HALF * s)
                    t = dve(lambda e, b=b, c=c: e.scalar_tensor_tensor(XT[:, c, :], PS[b][:, :], weight, XT[:, c, :],
                                                                       ALU.mult, ALU.add), p)
                    bank_free[b] = [t]
                    if s == 1:
                        if norm is not None:
                            norm.feed(c, t)
                        else:
                            dma(io["out"][:, c, :], XT[:, c, :], s_out, 16 * (c + 1), t)
                    tick()
                g_free[0] = p
            return p

        t_par = dma(PAR[:, :], io["par"], s_par, 16)
        t_const = dma(CONST[:, :], io["const"], s_const, 16)
        C0 = VA[:, 0, 0:640]
        t_x = dma(XT[:, :, :], io["x"], s_x, 16)
        t_c0 = dma(C0, io["cr"], s_cr, 16)
        W.load_to(NRAW - 1)
        MT = [MT0, MT1]
        t_mem = []
        for m in range(2):
            t_mem.append(dma(MT[m][:, :, :], io["mem"][m], s_mem, 16 * (m + 1), t_mem))
        t_cb = dma(CB[:, :], io["cb"], s_cb, 16)

        t_cr = act(lambda e: e.activation(CR[:, :], C0, ACT.Copy), t_c0)
        t_eps = pool(lambda e: e.memset(EPSC[:, 0:1], EPS))
        t_one = pool(lambda e: e.memset(EPSC[:, 1:2], 1.0))
        pool(lambda e: e.tensor_scalar(NSINK[:, :], par("sink", 0, n=8), -1.0, None, ALU.mult), t_par)
        t_gain = pool(lambda e: e.tensor_scalar(par("mq0", 0, n=5), par("mq0", 0, n=5), 0.125, None, ALU.mult), t_par)
        t_gain = pool(lambda e: e.tensor_scalar(par("mlaq"), par("mlaq"), 96.0 ** -0.5, None, ALU.mult), t_gain)
        act(lambda e: e.preload_act_table_set(TABLES), signal=False)

        def memories(p_in, norms):
            for nm in norms:
                nm.finish([p_in])
            for m in range(2):
                for c in range(4):
                    b, p, pp_ = norms[m].normed(("w_mem_kv", "w_mem_kv_2")[m], 0, 128 * c)
                    tick()
                    if c < 2:
                        dst = [(0, "mk0"), (1, "mk1")] if m == 0 else [(2, "gmk2")]
                        go(head_norm(b, p, MEM, 1 / 64, [(slice(0, 128), gn, KMEM[:, x, c, :]) for x, gn in dst],
                                     kv_got[m]))
                    else:
                        go(to_rows(b, p, MEM, lambda e, s, m=m, c=c: e.tensor_copy(
                            VMEM[:, m, :, 128 * (c - 2):128 * (c - 1)], s), kv_got[m]))
            return pp_

        kv_got = [[], []]
        norm = ColumnNorm(XT, "mix0", hn_free=[])
        norm.feed_all(t_x)

        def mem_items(i, m, km):
            return [Item(MQ[64 * (h % 2):64 * (h % 2) + 64, h // 2, 128 * i:128 * i + 128],
                         KMEM[64 * (h % 2):64 * (h % 2) + 64, km, h // 2, :], [], MEM,
                         [VMEM[:, m, k, 64 * h:64 * h + 64] for k in range(2)], 12 + h, [mix_got, kv_got[m]])
                    for h in range(4)]

        lo, hi = slice(0, 64), slice(64, 128)

        def go(g):
            try:
                next(g)
                start(g)
            except StopIteration:
                pass

        mix_got = []
        t_rope = []
        CUM = OT[0:12, 0:T]
        NCUM = OT[0:12, T:2 * T]
        tq = pool(lambda e: e.memset(QA[64:66, :, :], 1.0))
        tk = pool(lambda e: e.memset(KA[64:66, :, :], 1.0))

        def decay(b, p):
            f, A, fa = tmp.take()
            k, B, fb = tmp.take()
            j, C, fc = sq.take()
            r = slice(0, 12)
            z = dve(lambda e: e.tensor_scalar(A[r, :], PS[b][r, :], par("bf", 0, r), None, ALU.add), p, fa, t_par)
            bank_free[b] = [z]
            x = act(lambda e: e.activation(B[r, :], A[r, :], ACT.Abs), z, fb)
            y = act(lambda e: e.activation(B[r, :], B[r, :], ACT.Exp, scale=-1.0), x)
            y = act(lambda e: e.activation(B[r, :], B[r, :], ACT.Ln, bias=EPSC[r, 1:2]), y, t_one)
            o = dve(lambda e: e.memset(C[r, :], 1.0), fc)
            z = dve(lambda e: e.tensor_scalar(A[r, :], A[r, :], 0.0, None, ALU.min), z, x)
            z = dve(lambda e: e.tensor_tensor(A[r, :], A[r, :], B[r, :], ALU.subtract), z, y)
            z = dve(lambda e: e.tensor_tensor_scan(CUM, C[r, :], A[r, :], 0.0, ALU.mult, ALU.add), z, o)
            w = dve(lambda e: e.tensor_scalar(NCUM, CUM, -1.0, None, ALU.mult), z)
            tmp.free[f] = tmp.free[k] = [z]
            sq.free[j] = [z]
            mix_got.append(dma(QA[65:66, :, :], CUM, s_cum, 16, z, tq))
            mix_got.append(dma(KA[64:65, :, :], NCUM, s_cum, 32, w, tk, mix_got[-1]))

        mem_norms = [ColumnNorm(MT[m], ("memn", "memn2")[m], MEM, MEM * m, ACCM[:, m, :]) for m in range(2)]
        for n, c in enumerate(range(21)):
            b, p, done = norm.normed("fox", 0, 128 * c)
            tick()
            if c == 8:
                mem_norms[0].feed_all(t_mem[0])
            if c == 14:
                mem_norms[1].feed_all(t_mem[1])
            if c == 0:
                decay(b, p)
            elif c < 13:
                A, g, ch = (QA, "foxq", c - 1) if c < 7 else (KA, "foxk", c - 7)
                go(head_norm(b, p, T, 1 / 64, [(lo, g, A[0:64, 2 * ch, :]), (hi, g, A[0:64, 2 * ch + 1, :])], mix_got))
            elif c < 19:
                ch = c - 13
                go(to_rows(b, p, T, lambda e, s, ch=ch: e.tensor_copy(VA[:, :, 128 * ch:128 * ch + 128], s), mix_got))
            else:
                go(head_norm(b, p, T, 1 / 64, [(slice(0, 128), "mq0", MQ[:, c - 19, :])], mix_got))
        p = memories(done, mem_norms)
        flush()

        def full_tiles(rows, m, km):
            return [[Item(QA[rows, h, 128 * i:128 * i + 128], KA[rows, h, 0:128 * (i + 1)], [(128 * i, MCAUS)],
                          128 * (i + 1), [VA[:, k, 64 * h:64 * h + 64] for k in range(i + 1)], h, mix_got)
                     for h in range(12)] + mem_items(i, m, km) for i in range(4)]

        chunk_map[0] = lambda c: c
        got = attention(full_tiles(slice(0, 66), 0, 0), [p])
        norm = ColumnNorm(XT, "nf0")
        p = project("w_out", 0, got, norm)
        norm.finish([p])
        last, norm = norm, ColumnNorm(XT, "mix1")
        p = ffn("ffn_w_up", "ffn_w_up", "ffn_w_down", 0, FF, last, True, 1.0, norm)
        act(lambda e: e.preload_act_table_set(TABLES), signal=False)

        mix_got = []
        t_rope.clear()

        def tables():
            i, PF, free = tmp.take()
            t_pos = []
            for m in range(2):
                pool(lambda e, m=m: e.dma_start(POS[m], io["pos"][m]).then_inc(s_pos, 16), p, signal=False)
                t_pos.append((s_pos, 16 * (m + 1)))
            A, N, NF = (VA[:, k, 0:T] for k in (1, 2, 3))
            NI = N.bitcast(I32)
            last = []
            for w in range(2):
                z = dve(lambda e, w=w: e.tensor_copy(PF[:, :], POS[w]), t_pos, free, last)
                a = dve(lambda e, w=w: e.tensor_scalar(A, PF[:, :], par(f"fr{w}"), None, ALU.mult), z, t_par, last)
                for k, quarter in ((0, 0.25), (1, 0.0)):
                    x = dve(lambda e, q=quarter: e.tensor_scalar(NI, A, 1 / (2 * PI), q, ALU.mult, ALU.add), a, last)
                    x = dve(lambda e: e.tensor_copy(NF, NI), x)
                    R = ROPE[:, 2 * w + k, :]
                    x = dve(lambda e, R=R: e.scalar_tensor_tensor(R, NF, -C1, A, ALU.mult, ALU.add), x)
                    x = dve(lambda e, R=R: e.scalar_tensor_tensor(R, NF, -C2, R, ALU.mult, ALU.add), x)
                    x = dve(lambda e, R=R: e.scalar_tensor_tensor(R, NF, -C3, R, ALU.mult, ALU.add), x)
                    x = dve(lambda e, R=R, q=quarter: e.tensor_scalar(R, R, 2 * PI * q, PI, ALU.add, ALU.min), x)
                    x = dve(lambda e, R=R: e.tensor_scalar(R, R, -PI, None, ALU.max), x)
                    last = [x]
                    t_rope.append(x)
            tmp.free[i] = last
            x = None
            for k in range(4):
                R = ROPE[:, k, :]
                x = act(lambda e, R=R: e.activation(R, R, ACT.Sin), t_rope[k])
            t_rope[:] = [x]
            act(lambda e: e.preload_act_table_set(TABLES), signal=False)
            return last

        POS = [VA[:, 0, 0:T].bitcast(I32), OT[:, 0:T].bitcast(I32)]
        t_va = tables()
        lat, krd = [], []
        banks = []
        for c in range(6):
            b, p, p_in = norm.normed("mla", 0, 128 * c)
            tick()
            banks.append((b, p))
            if c == 2:
                i, KR, free = tmp.take()
                a = act(lambda e, b=b: e.activation(KR[:, :], PS[b][:, :], ACT.Copy), p, free)
                bank_free[b] = [a]
            if c < 2:
                go(head_norm(b, p, T, 1 / 64, [(slice(0, 128), "mq1", MQ[:, c, :])], mix_got))
        flush()
        kr = []
        KRR = OT[:, 0:T]
        p_rot = rope(KR[:, :], a, 0, PM, [(slice(0, 128), KRR)], kr)
        tmp.free[i] = [p_rot, kr[-1]]
        tk = pool(lambda e: e.tensor_copy(KA[64:96, :, :], KRR[64:96].unsqueeze(1).broadcast_to([32, 12, T])), kr)
        def latent_norm(chunks, gain, scale):
            bb = aux_bank()
            for n, c in enumerate(chunks):
                b, pc = banks[3 + c]
                j, S, free = sq.take()
                a = act(lambda e, b=b, S=S: e.activation(S[:, :], PS[b][:, :], ACT.Square), pc, free)
                p = pe(lambda e, n=n, S=S: e.matmul(PS[bb][:, :], ONES, S[:, :], start=(n == 0),
                                                    stop=(n == len(chunks) - 1)), a, bank_free[bb] if n == 0 else [])
                sq.free[j] = [p]
            i, R, a = rsqrt(bb, slice(0, 128), T, scale, p)
            for n, c in enumerate(chunks):
                b, pc = banks[3 + c]
                k, B, free = tmp.take()
                g = dve(lambda e, b=b, B=B, n=n: e.scalar_tensor_tensor(B[:, :], PS[b][:, :], par(gain, n), R[:, :],
                                                                        ALU.mult, ALU.mult), a, pc, free)
                bank_free[b] = [g]
                t = split(B[:, :], HNh[:, c, :], HNl[:, c, :], g, p_in)
                tmp.free[k] = t
                lat.append((HNh[:, c, :], HNl[:, c, :], t))
            rs.free[i] = [g]

        latent_norm((0, 1), "qa", 1 / 256)
        latent_norm((2,), "kva", 1 / 128)

        q_raw = [[] for _ in range(12)]
        k_raw = [[tk] for _ in range(12)]

        def copies(b, p, A, c, raw):
            x = act(lambda e: e.activation(A[0:64, 2 * c, :], PS[b][0:64, :], ACT.Copy), p)
            y = dve(lambda e: e.tensor_copy(A[0:64, 2 * c + 1, :], PS[b][64:128, :]), p)
            raw[2 * c].append(x)
            raw[2 * c + 1].append(y)
            bank_free[b] = [x, y]

        def rope_chunk(b, p, r):
            i, B, free = tmp.take()
            a = act(lambda e: e.activation(B[:, :], PS[b][:, :], ACT.Copy), p, free)
            bank_free[b] = [a]
            yield
            res = []
            x = rope(B[:, :], a, 0, PM, [(slice(32 * j, 32 * j + 32), QA[64:96, 4 * r + j, :]) for j in range(4)], res)
            tmp.free[i] = [x, res[-1]]
            for j in range(4):
                q_raw[4 * r + j].append(res[j])

        summed = [0, None]

        def sum96(A, h, raw):
            r = slice(0, 96)
            j, S, free = sq.take()
            row = summed[0]
            summed[0] += 1
            if A is KA:
                a = pool(lambda e: e.tensor_tensor(S[r, :], A[r, h, :], A[r, h, :], ALU.mult), raw, free)
            else:
                a = act(lambda e: e.activation(S[r, :], A[r, h, :], ACT.Square), raw, free)
            w, (SQH, SQL), free = sq_parts.take()
            t = split(S[r, :], SQH[r, :], SQL[r, :], a, free)
            sq.free[j] = t
            yield
            pe(lambda e: e.matmul(PS[7][:, :], to_row(row)[r, :], SQH[r, :], start=(row == 0), stop=False), t, t_cr,
               bank_free[7] if row == 0 else [], signal=False)
            summed[1] = pe(lambda e: e.matmul(PS[7][:, :], to_row(row)[r, :], SQL[r, :], start=False,
                                              stop=(row == 23)))
            sq_parts.free[w] = [summed[1]]

        def scale96():
            r = slice(0, 24)
            j, S, free = sq.take()
            i, R, free2 = rs.take()
            w, (RH, RL), free3 = sq_parts.take()
            x = dve(lambda e: e.tensor_scalar(S[r, :], PS[7][r, :], 1 / 96, EPS, ALU.mult, ALU.add), summed[1], free)
            bank_free[7] = [x]
            y = act(lambda e: e.activation(R[r, :], S[r, :], ACT.Ln), x, free2)
            y = act(lambda e: e.activation(R[r, :], R[r, :], ACT.Exp, scale=-0.5), y)
            z = dve(lambda e: e.tensor_tensor(S[r, :], S[r, :], R[r, :], ALU.mult), y)
            z = dve(lambda e: e.scalar_tensor_tensor(S[r, :], S[r, :], -0.5, R[r, :], ALU.mult, ALU.mult), z)
            z = dve(lambda e: e.scalar_tensor_tensor(R[r, :], S[r, :], 1.5, R[r, :], ALU.add, ALU.mult), z)
            t = split(R[r, :], RH[r, :], RL[r, :], z, free3)
            sq.free[j] = rs.free[i] = t
            r96 = slice(0, 96)
            for row in range(24):
                A, h, gain, raw = (KA, row, "mlak", k_raw) if row < 12 else (QA, row - 12, "mlaq", q_raw)
                b = (5, 6, 3, 4)[row % 4]
                lhs = IDENTR[r, row:row + 1].broadcast_to([24, 128])
                pe(lambda e, b=b, lhs=lhs: e.matmul(PS[b][:, :], lhs, RH[r, :], start=True, stop=False), t,
                   bank_free[b], signal=False)
                p = pe(lambda e, b=b, lhs=lhs: e.matmul(PS[b][:, :], lhs, RL[r, :], start=False, stop=True))
                g = dve(lambda e, A=A, h=h, gain=gain, b=b: e.scalar_tensor_tensor(
                    A[r96, h, :], A[r96, h, :], par(gain, 0, r96), PS[b][r96, :], ALU.mult, ALU.mult),
                    p, raw[h], t_gain)
                bank_free[b] = [g]
            sq_parts.free[w] = [p]
            mix_got.append(g)

        for c in range(9):
            b, p = dense("mla_q", 0, 128 * c, lat[0:2])
            tick()
            if c < 6:
                copies(b, p, QA, c, q_raw)
            else:
                go(rope_chunk(b, p, c - 6))
        flush()
        for c in range(12):
            b, p = dense("mla_kv", 0, 128 * c, lat[2:3])
            tick()
            if c < 6:
                copies(b, p, KA, c, k_raw)
                go(sum96(KA, 2 * c, k_raw[2 * c]))
                go(sum96(KA, 2 * c + 1, k_raw[2 * c + 1]))
            else:
                ch = c - 6
                go(to_rows(b, p, T, lambda e, s, ch=ch: e.tensor_copy(VA[:, :, 128 * ch:128 * ch + 128], s), mix_got))
                go(sum96(QA, 2 * ch, q_raw[2 * ch]))
                go(sum96(QA, 2 * ch + 1, q_raw[2 * ch + 1]))
        flush()
        scale96()
        got = attention(full_tiles(slice(0, 96), 0, 1), [p])
        norm = ColumnNorm(XT, "nf1")
        p = project("w_out", 1, got, norm)
        norm.finish([p])
        last, norm = norm, ColumnNorm(XT, "f1")
        p = ffn("ffn_w_up", "ffn_w_up", "ffn_w_down", 1, FF, last, True, 1.0, norm)
        act(lambda e: e.preload_act_table_set(TABLES), signal=False)

        last, norm = norm, ColumnNorm(XT, "mix2")
        p = ffn("w_ffn1_gate_2", "w_ffn1_up_2", "w_ffn1_down_2", 0, 0, last, False, 0.5, norm)
        act(lambda e: e.preload_act_table_set(TABLES), signal=False)

        mix_got = []
        HP = KA[:, 0:4, :].rearrange("p h t -> p (h t)")
        HW = T + 30
        HX = [HP[:, 0:HW], HP[:, HW:2 * HW]]
        CA = [KA[:, 4, :], KA[:, 5, :]]
        SG = [KA[:, 6, :], KA[:, 7, :]]
        zero = [pool(lambda e, c=c: e.memset(HX[c][:, 0:30], 0.0), p) for c in range(2)]
        q_rot = [[] for _ in range(5)]

        def rotated(n):
            res = []
            yield
            yield
            rope(QA[:, n, :], q_rot[n], 1, PB, [(slice(0, 128), QA[:, n, :])], res)
            mix_got.extend(res)

        glu = {}

        conv_done = []
        attending = [True]

        def conformer():
            t = [None, None]
            for n in range(2):
                t[n] = dve(lambda e, n=n: e.tensor_scalar(CA[n], HX[n][:, 30:30 + T], par("dw", 31 * n + 30),
                                                          par("db", n), ALU.mult, ALU.add), glu[n])
                for k in range(30):
                    if k % 2 == 0:
                        yield
                    t[n] = dve(lambda e, n=n, k=k: e.scalar_tensor_tensor(CA[n], HX[n][:, k:k + T], par("dw", 31 * n + k),
                                                                          CA[n], ALU.mult, ALU.add), t[n])
            while attending[0]:
                yield
            b = 5
            for n in range(2):
                p = pe(lambda e, n=n: e.matmul(PS[b][:, :], ONES, CA[n], start=(n == 0), stop=(n == 1)), t,
                       bank_free[b] if n == 0 else [])
            for n in range(2):
                t[n] = dve(lambda e, n=n: e.scalar_tensor_tensor(CA[n], PS[b][:, :], -1 / 256, CA[n], ALU.mult,
                                                                 ALU.add), p, t[n])
            bank_free[b] = [t[1]]
            a = []
            for n in range(2):
                a.append(act(lambda e, n=n: e.activation(SG[n], CA[n], ACT.Square), t[n]))
            for n in range(2):
                p = pe(lambda e, n=n: e.matmul(PS[b][:, :], ONES, SG[n], start=(n == 0), stop=(n == 1)), a,
                       bank_free[b] if n == 0 else [])
            j, R, x = rsqrt(b, slice(0, 128), T, 1 / 256, p)
            for n in range(2):
                t[n] = dve(lambda e, n=n: e.scalar_tensor_tensor(CA[n], CA[n], par("lg", n), R[:, :], ALU.mult,
                                                                 ALU.mult), x, t[n])
            rs.free[j] = [t[1]]
            conv_done.extend(t)

        for c in range(12):
            b, p, p_in = norm.normed("w_in_2", 0, 128 * c)
            tick()
            if c < 2:
                a = act(lambda e, b=b, c=c: e.activation(SG[c], PS[b][:, :], ACT.Sigmoid), p)
                bank_free[b] = [a]
                glu[c] = a
                if c == 1:
                    act(lambda e: e.preload_act_table_set(TABLES), signal=False)
            elif c < 4:
                n = c - 2
                t = dve(lambda e, b=b, n=n: e.tensor_tensor(HX[n][:, 30:30 + T], PS[b][:, :], SG[n], ALU.mult),
                        p, glu[n], zero)
                bank_free[b] = [t]
                glu[n] = t
                if n == 1:
                    slow.append(conformer())
            elif c < 9:
                n = c - 4
                go(head_norm(b, p, T, 1 / 64, [(slice(0, 128), "gq2" if n < 4 else "gk2", QA[:, n, :])], q_rot[n]))
                go(rotated(n))
            elif c == 9:
                go(to_rows(b, p, T, lambda e, s: e.tensor_copy(VA[:, :, 0:128], s), mix_got))
            else:
                go(head_norm(b, p, T, 1 / 64, [(slice(0, 128), "gmq2", MQ[:, c - 10, :])], mix_got))
        flush()

        blk = []
        for i in range(4):
            k0 = max(0, i - 1)
            nk = 128 * (i + 1 - k0)
            masks = [(0, MPREV), (128, MCAUS)] if i else [(0, MCAUS)]
            items = []
            for h in range(8):
                r = lo if h < 4 else hi
                items.append(Item(QA[r, h % 4, 128 * i:128 * i + 128], QA[r, 4, 128 * k0:128 * k0 + nk], masks, nk,
                                  [VA[:, k0 + k, 64 * (h // 4):64 * (h // 4) + 64] for k in range(nk // 128)],
                                  h, mix_got, sink=h))
            mem = mem_items(i, 1, 2)
            for it in mem:
                it.slot -= 4
            blk.append(items + mem)
        chunk_map[0] = lambda c: c if c < 4 else c + 2
        attending[0] = True
        got = attention(blk, [p_in])
        attending[0] = False
        while slow:
            tick()
        for n in range(2):
            a = act(lambda e, n=n: e.activation(SG[n], CA[n], ACT.Silu, bias=par("lb", n)), conv_done)
            got.extend(split(SG[n], HNh[:, 4 + n, :], HNl[:, 4 + n, :], a, p_in))
        act(lambda e: e.preload_act_table_set(TABLES), signal=False)
        norm = ColumnNorm(XT, "f2")
        p = project("w_out_2", 0, got, norm)
        norm.finish([p])
        ffn("w_ffn2_gate_2", "w_ffn2_up_2", "w_ffn2_down_2", 0, 0, norm, False, 0.5, None)
        sp.wait((s_out, 16 * KC))
        assert W.at == len(plan)

        block = ctx.enter_context(nc.Block())
        block.tensor(pe.play)
        block.vector(dve.play)
        block.scalar(act.play)
        block.gpsimd(pool_q.play)
        block.sync(sp.play)


def lay_out(x):
    f = {k: np.asarray(v) for k, v in x.items()}
    fox = f["fox_w_in"][0]
    pad = np.zeros((D, 116), fox.dtype)
    mla = f["mla_w_in"][0]
    kr = mla[:, 384:416]
    qu = f["mla_w_q_up"][0].reshape(256, 12, 96)
    kvu = f["mla_w_kv_up"][0].reshape(128, 12, 128)
    w2 = f["w_in_2"][0]
    q2 = w2[:, 0:512].reshape(D, 2, 4, 64).transpose(0, 2, 1, 3).reshape(D, 512)
    src = {
        "w_mem_kv": f["w_mem_kv"], "w_mem_kv_2": f["w_mem_kv_2"][0],
        "fox": np.concatenate([fox[:, 2304:2316], pad, fox[:, :2304], fox[:, 2316:]], 1),
        "mla": np.concatenate([mla[:, 416:], kr, kr, kr, kr, mla[:, :384]], 1),
        "mla_q": np.concatenate([qu[:, :, :64].reshape(256, 768), qu[:, :, 64:].reshape(256, 384)], 1),
        "mla_kv": np.concatenate([kvu[:, :, :64].reshape(128, 768), kvu[:, :, 64:].reshape(128, 768)], 1),
        "w_in_2": np.concatenate([w2[:, 1024:1280], w2[:, 768:1024], q2, w2[:, 512:768], w2[:, 1280:]], 1),
    }

    def tile(key):
        name, layer, r, c = key
        a = src[name] if name in src else f[name][layer]
        return a[r:r + 128, c:c + 128]

    plan = weight_plan()
    n = (len(plan) + UT - 1) // UT
    w = np.zeros((n, 128, 128 * UT), np.float32)
    for i, key in enumerate(plan):
        w[i // UT, :, 128 * (i % UT):128 * (i % UT) + 128] = tile(key)

    def cols(a):
        return a.reshape(-1, 128).T

    def twice(a):
        return np.concatenate([a, a]).reshape(128, 1)

    def rows(a):
        return np.concatenate([a, np.zeros(128 - a.size, a.dtype)]).reshape(128, 1)

    fr0 = (10000.0 ** (-np.arange(0, 32, 2) / 32)).astype(np.float32)
    fr1 = (500000.0 ** (-np.arange(8) / 8)).astype(np.float32)
    half = np.concatenate([fr1, fr1, np.zeros(48, np.float32)])
    p = {
        "mix0": cols(f["norm_mix"][0]), "mix1": cols(f["norm_mix"][1]), "nf0": cols(f["norm_ffn"][0]),
        "nf1": cols(f["norm_ffn"][1]), "memn": cols(f["mem_norm"]), "f1": cols(f["g_ffn1_2"][0]),
        "mix2": cols(f["g_mix_2"][0]), "memn2": cols(f["g_mem_2"][0]), "f2": cols(f["g_ffn2_2"][0]),
        "mq0": twice(f["mem_q_gain"][0]), "mq1": twice(f["mem_q_gain"][1]), "foxq": twice(f["fox_q_gain"][0]),
        "gq2": twice(f["g_q_2"][0]), "gmq2": twice(f["g_mq_2"][0]), "mlaq": rows(f["mla_q_gain"][0]),
        "mk0": twice(f["mem_k_gain"][0]), "mk1": twice(f["mem_k_gain"][1]), "foxk": twice(f["fox_k_gain"][0]),
        "gk2": twice(f["g_k_2"][0]), "gmk2": twice(f["g_mk_2"][0]), "mlak": rows(f["mla_k_gain"][0]),
        "qa": cols(f["mla_qa_norm"][0]), "kva": cols(f["mla_kva_norm"][0]), "bf": rows(f["fox_b_f"][0]),
        "db": cols(f["b_dw_2"][0]), "lg": cols(f["g_conv_ln_2"][0]), "lb": cols(f["b_conv_ln_2"][0]),
        "dw": f["w_dw_2"][0].reshape(31, 2, 128).transpose(2, 1, 0).reshape(128, 62),
        "sink": np.broadcast_to(f["sinks_2"][0], (128, 8)),
        "fr0": np.tile(fr0, 8).reshape(128, 1), "fr1": np.concatenate([half, half]).reshape(128, 1),
    }
    for i in range(2):
        p[f"cw{i}"] = f["ffn_conv_w"][i].reshape(3, 44, 128).transpose(2, 1, 0).reshape(128, 132)
        p[f"cb{i}"] = cols(f["ffn_conv_b"][i])
    parts = [p[name] for name, _ in PARAMS]

    def chunks(a):
        return a.T.reshape(8, 128, -1).transpose(1, 0, 2)

    eye = np.eye(128, dtype=np.float32)
    blk = np.kron(np.eye(2), np.ones((64, 64)))

    def rot(width, half):
        m = np.zeros((128, 128))
        for g in range(0, 128, width):
            for j in range(half):
                m[g + j + half, g + j] = -1.0
                m[g + j, g + j + half] = 1.0
        return m

    const = np.concatenate([eye, np.ones((128, 128)), rot(32, 16), rot(64, 8)], 1).astype(np.float32)
    col = np.zeros((128, 256))
    col[:, 127] = 1.0
    cr = np.concatenate([np.ones((128, 128)), blk, eye, col], 1).astype(np.float32)
    q, k = np.arange(128)[:, None], np.arange(128)[None, :]
    cb = np.concatenate([eye, np.where(k <= q, 0.0, NEG), np.where(k > q, 0.0, NEG)], 1).astype(mybir.dt.np(BF16))
    return {
        "w": w, "par": np.concatenate(parts, 1), "const": const, "cr": cr, "cb": cb,
        "x": chunks(f["x"][0]), "mem": np.stack([chunks(f["mem"][0]), chunks(f["mem_2"][0])]),
        "pos": np.stack([np.broadcast_to(f[k][0], (128, T)) for k in ("positions", "positions_2")]),
    }


def kernel(**inputs):
    import concourse.bacc as bacc
    from concourse.bass_utils import run_bass_kernel_spmd as run

    nc = bacc.Bacc("TRN2", target_bir_lowering=False, num_devices=1)
    laid = {k: np.ascontiguousarray(v) for k, v in lay_out(inputs).items()}
    io = {k: nc.dram_tensor(f"in_{k}", v.shape, mybir.dt.from_np(v.dtype), kind="ExternalInput").ap()
          for k, v in laid.items()}
    io["out"] = nc.dram_tensor("out_x", (128, KC, T), F32, kind="ExternalOutput").ap()
    program(nc, io)
    r = run(nc, [{f"in_{k}": v for k, v in laid.items()}], core_ids=[0])
    got = r.results[0]["out_x"]
    return np.ascontiguousarray(got.transpose(1, 0, 2).reshape(D, T).T)[None]
```

```python
from contextlib import ExitStack

import numpy as np
from concourse import mybir

F32 = mybir.dt.float32
F32R = mybir.dt.float32r
BF16 = mybir.dt.bfloat16
I32 = mybir.dt.int32
ALU = mybir.AluOpType
ACT = mybir.ActivationFunctionType
AX = mybir.AxisListType.X

T = 512
MEM = 256
D = 1024
KC = D // 128
FF = 2816
FC = FF // 128
HALF = FC // 2
EPS = 1e-6
NEG = -1.0e30
UT = 4
NRAW = 6
NSPL = 5
AHEAD = 3
TABLES = "natural_log_exp_and_others"
PI = float(np.pi)
C1 = 6.28125
C2 = float(np.float32(int((2 * np.pi - C1) * 2 ** 20) / 2 ** 20))
C3 = float(2 * np.pi - C1 - C2)


def weight_plan():
    t = []

    def out(name, layer, col, rows=8, row0=0):
        for k in range(rows):
            t.append((name, layer, row0 + 128 * k, col))

    def ffn(gate, up, down, layer, off):
        for s in range(2):
            for p in range(HALF):
                c = 128 * (HALF * s + p)
                out(gate, layer, c)
                out(up, layer, off + c)
            for c in range(8):
                out(down, layer, 128 * c, HALF, 128 * HALF * s)

    for c in range(21):
        out("fox", 0, 128 * c)
    for name in ("w_mem_kv", "w_mem_kv_2"):
        for c in range(4):
            out(name, 0, 128 * c)
    for c in range(8):
        out("w_out", 0, 128 * c)
    ffn("ffn_w_up", "ffn_w_up", "ffn_w_down", 0, FF)
    for c in range(6):
        out("mla", 0, 128 * c)
    for c in range(9):
        out("mla_q", 0, 128 * c, 2)
    for c in range(12):
        out("mla_kv", 0, 128 * c, 1)
    for c in range(8):
        out("w_out", 1, 128 * c)
    ffn("ffn_w_up", "ffn_w_up", "ffn_w_down", 1, FF)
    ffn("w_ffn1_gate_2", "w_ffn1_up_2", "w_ffn1_down_2", 0, 0)
    for c in range(12):
        out("w_in_2", 0, 128 * c)
    for c in range(8):
        out("w_out_2", 0, 128 * c)
    ffn("w_ffn2_gate_2", "w_ffn2_up_2", "w_ffn2_down_2", 0, 0)
    return t


PARAMS = [("mix0", 8), ("mix1", 8), ("nf0", 8), ("nf1", 8), ("memn", 8), ("f1", 8), ("mix2", 8), ("memn2", 8),
          ("f2", 8), ("mq0", 1), ("mq1", 1), ("foxq", 1), ("gq2", 1), ("gmq2", 1), ("mlaq", 1),
          ("mk0", 1), ("mk1", 1), ("foxk", 1), ("gk2", 1), ("gmk2", 1), ("mlak", 1), ("qa", 2), ("kva", 1),
          ("bf", 1), ("cw0", 132), ("cb0", 44), ("cw1", 132), ("cb1", 44), ("dw", 62), ("db", 2), ("lg", 2),
          ("lb", 2), ("sink", 8), ("fr0", 1), ("fr1", 1)]


def param_plan():
    at, n = {}, 0
    for name, k in PARAMS:
        at[name] = n
        n += k
    return at, n


class Queue:

    def __init__(self, sem):
        self.sem, self.ops, self.n, self.seen = sem, [], 0, {}

    def __call__(self, fn, *after, signal=True):
        self.wait(*after)
        self.ops.append((fn, self.sem if signal else None))
        if signal:
            self.n += 1
        return (self.sem, self.n) if signal else None

    def wait(self, *after):
        for a in after:
            if isinstance(a, list):
                self.wait(*a)
            elif a is not None and self.seen.get(a[0], 0) < a[1]:
                self.seen[a[0]] = a[1]
                self.ops.append((None, a))

    def play(self, eng):
        for fn, what in self.ops:
            if fn is None:
                eng.wait_ge(*what)
            else:
                ins = fn(eng)
                if what is not None:
                    ins.then_inc(what, 1)


class Ring:

    def __init__(self, items):
        self.items, self.free, self.at = items, [[] for _ in items], -1

    def take(self):
        self.at = (self.at + 1) % len(self.items)
        return self.at, self.items[self.at], self.free[self.at]


def program(nc, io):
    with ExitStack() as ctx:
        def sb(name, shape, dt=F32):
            return ctx.enter_context(nc.sbuf_tensor(name, shape, dt))

        def sem(name):
            return ctx.enter_context(nc.semaphore(name))

        PA, NPAR = param_plan()
        plan = weight_plan()
        n_units = (len(plan) + UT - 1) // UT

        pe, dve, act, pool_q, sp = (Queue(sem(n)) for n in ("s_pe", "s_dve", "s_act", "s_pool", "s_sp"))
        s_raw = [sem(f"s_raw{i}") for i in range(NRAW)]

        def pool(fn, *after, signal=True):
            return pool_q(fn, (pool_q.sem, pool_q.n) if pool_q.n else None, *after, signal=signal)

        def dma(dst, src, s, count, *after):
            sp.wait(*after)
            sp.ops.append((lambda e: e.dma_start(dst, src).then_inc(s, 16), None))
            return (s, count)

        XT = sb("XT", [128, KC, T])
        HNh = sb("HNh", [128, KC, T], F32R)
        HNl = sb("HNl", [128, KC, T], F32R)
        RAW = [sb(f"RAW{i}", [128, 128 * UT]) for i in range(NRAW)]
        WH = [sb(f"WH{i}", [128, 128 * UT], F32R) for i in range(NSPL)]
        WL = [sb(f"WL{i}", [128, 128 * UT], F32R) for i in range(NSPL)]
        PAR = sb("PAR", [128, NPAR])
        CONST = sb("CONST", [128, 512])
        IDENT, ONES, PM, PB = (CONST[:, 128 * i:128 * i + 128] for i in range(4))
        CB = sb("CB", [128, 384], BF16)
        IDB, MCAUS, MPREV = (CB[:, 128 * i:128 * i + 128] for i in range(3))
        CR = sb("CR", [128, 640], F32R)
        ONESR, BLKR, IDENTR = (CR[:, 128 * i:128 * i + 128] for i in range(3))

        def to_row(h):
            return CR[:, 384 + 127 - h:384 + 255 - h]
        sq_parts = Ring([(sb(f"SQH{i}", [128, T], F32R), sb(f"SQL{i}", [128, T], F32R)) for i in range(2)])
        ACC = sb("ACC", [128, T])
        EPSC = sb("EPSC", [128, 2])
        early = ExitStack()
        MT0 = early.enter_context(nc.sbuf_tensor("MT0", [128, 8, MEM], F32))
        early.close()
        ROPE = sb("ROPE", [128, 4, T])
        KMEM = sb("KMEM", [128, 3, 2, MEM])
        VMEM = sb("VMEM", [128, 2, 2, MEM])
        stats = Ring([sb(f"STAT{i}", [128, 4, 4]) for i in range(3)])
        NSINK = sb("NSINK", [128, 8])
        rs = Ring([sb(f"RS{i}", [128, T]) for i in range(2)])
        sq = Ring([sb(f"SQ{i}", [128, T]) for i in range(2)])
        tmp = Ring([sb(f"TMP{i}", [128, T]) for i in range(3)])
        base = nc.sbuf_base
        mixer = ExitStack()

        def mb(name, shape, dt=F32, stack=mixer):
            return stack.enter_context(nc.sbuf_tensor(name, shape, dt))

        QA = mb("QA", [128, 12, T])
        KB = mb("KB", [128, 4, T])
        VA = mb("VA", [128, 4, 768])
        MQ = mb("MQ", [128, 2, T])
        parts_of = Ring([tuple(mb(f"{n}{i}", [128, T], F32R) for n in ("QH", "QL", "KH", "KL")) for i in range(2)])
        early = ExitStack()
        MT1 = early.enter_context(nc.sbuf_tensor("MT1", [128, 8, MEM], F32))
        ACCM = early.enter_context(nc.sbuf_tensor("ACCM", [128, 2, MEM], F32))
        early.close()
        pp = Ring([mb(f"PP{i}", [128, T]) for i in range(4)])
        pt = Ring([mb(f"PT{i}", [128, T]) for i in range(3)])
        ot = Ring([x[:, :].rearrange("p (i f) -> p i f", f=128) for x in tmp.items[0:2]])

        def key_rows(r, h):
            return XT[r, h, :] if h < 8 else KB[r, h - 8, :]
        mixer.close()
        ffn_mem = ExitStack()
        Gh = mb("Gh", [128, HALF, T], F32R, ffn_mem)
        Gl = mb("Gl", [128, HALF, T], F32R, ffn_mem)
        cv = Ring([mb(f"CV{i}", [128, T], F32, ffn_mem) for i in range(4)])
        gf = Ring([mb(f"GF{i}", [128, T], F32, ffn_mem) for i in range(2)])
        ffn_mem.close()

        PS = [ctx.enter_context(nc.psum_tensor(f"PS{i}", [128, T], F32)) for i in range(8)]
        bank_free = [[] for _ in range(8)]

        def par(name, i=0, rows=slice(0, 128), n=1):
            a = PA[name] + i
            return PAR[rows, a:a + n]

        s_par, s_const, s_cb, s_pos, s_x, s_mem = (sem(n) for n in ("s_par", "s_const", "s_cb", "s_pos", "s_x", "s_mem"))
        s_cum, s_out, s_cr = sem("s_cum"), sem("s_out"), sem("s_cr")
        s_spill, s_fill = sem("s_spill"), sem("s_fill")

        class Weights:
            def __init__(self):
                self.at = 0
                self.raw_free = {}
                self.used = {}
                self.loaded = -1
                self.ready = {}

            def load_to(self, u):
                while self.loaded < min(u, n_units - 1):
                    self.loaded += 1
                    v = self.loaded
                    dma(RAW[v % NRAW][:, :], io["w"][v], s_raw[v % NRAW], 16 * (v // NRAW + 1),
                        self.raw_free.get(v - NRAW))

            def prepare(self, u):
                if u >= n_units or u in self.ready:
                    return
                r, h, l = RAW[u % NRAW], WH[u % NSPL], WL[u % NSPL]
                landed = (s_raw[u % NRAW], 16 * (u // NRAW + 1))
                a = act(lambda e: e.activation(h[:, :], r[:, :], ACT.Copy), landed, self.used.get(u - NSPL))
                b = dve(lambda e: e.tensor_tensor(l[:, :], r[:, :], h[:, :], ALU.subtract), landed, a,
                        self.used.get(u - NSPL))
                self.raw_free[u] = [a, b]
                self.ready[u] = [a, b]
                self.load_to(u + NRAW)

            def tile(self, key):
                assert plan[self.at] == key, (plan[self.at], key)
                u, j = divmod(self.at, UT)
                if j == 0:
                    for v in range(u, u + AHEAD + 1):
                        self.prepare(v)
                self.at += 1
                last = j == UT - 1 or self.at == len(plan)
                c = slice(128 * j, 128 * j + 128)
                return WH[u % NSPL][:, c], WL[u % NSPL][:, c], self.ready[u], (u if last else None)

        W = Weights()

        tasks = []

        slow = []

        soon, late = [], []

        def end_soon():
            while soon:
                soon.pop(0)()

        def end_late():
            end_soon()
            while late:
                late.pop(0)()

        def tick():
            end_late()
            for some in (tasks, slow):
                for t in list(some):
                    try:
                        next(t)
                    except StopIteration:
                        some.remove(t)

        def start(t):
            tasks.append(t)

        def flush():
            while tasks or soon or late:
                tick()

        dense_at = [0]

        def dense(name, layer, col, rhs, N=T, row0=0, banks=(0, 1, 2, 3, 4)):
            end_soon()
            b = banks[dense_at[0] % len(banks)]
            dense_at[0] += 1
            pe.wait(bank_free[b])
            n = len(rhs)
            for k, (xh, xl, got) in enumerate(rhs):
                wh, wl, ready, last = W.tile((name, layer, row0 + 128 * k, col))
                out = PS[b][:, 0:N]
                pe(lambda e, o=out, a=wh, x=xh, k=k: e.matmul(o, a, x, start=(k == 0), stop=False),
                   ready, got, signal=False)
                pe(lambda e, o=out, a=wh, x=xl: e.matmul(o, a, x, start=False, stop=False), signal=False)
                t = pe(lambda e, o=out, a=wl, x=xh, k=k: e.matmul(o, a, x, start=False, stop=(k == n - 1)),
                       signal=(last is not None or k == n - 1))
                if last is not None:
                    W.used[last] = t
            end_late()
            return b, t

        def split(src, h, l, *after):
            a = act(lambda e: e.activation(h, src, ACT.Copy), *after)
            b = dve(lambda e: e.tensor_tensor(l, src, h, ALU.subtract), a, *after)
            return [a, b]

        def rsqrt(bank, rows, N, scale, done):
            j, R, free = rs.take()
            a = act(lambda e: e.activation(R[rows, 0:N], PS[bank][rows, 0:N], ACT.Ln, bias=EPSC[rows, 0:1],
                                           scale=scale), done, free, t_eps)
            bank_free[bank] = [a]
            a = act(lambda e: e.activation(R[rows, 0:N], R[rows, 0:N], ACT.Exp, scale=-0.5), a)
            return j, R, a

        aux = [0]

        def aux_bank():
            aux[0] += 1
            return 5 + aux[0] % 2

        class ColumnNorm:

            def __init__(self, X, gain, N=T, at=0, acc=None, hn_free=None):
                self.X, self.gain, self.N, self.at0, self.n = X, gain, N, at, 0
                self.acc, self.hn_free = (ACC[:, :] if acc is None else acc), hn_free
                self.out, self.fed, self.r = [], [], None

            def part(self, c, token, hn_free):
                N, o = self.N, self.at0
                h, l = HNh[:, c, o:o + N], HNl[:, c, o:o + N]
                a = act(lambda e: e.activation(h, self.X[:, c, 0:N], ACT.Copy, scale=par(self.gain, c)), token,
                        hn_free, t_par)
                b = dve(lambda e: e.scalar_tensor_tensor(l, self.X[:, c, 0:N], par(self.gain, c), h, ALU.mult,
                                                         ALU.subtract), a, token, hn_free, t_par)
                self.out.append((h, l, [a, b]))

            def feed(self, c, token):
                N = self.N
                if self.hn_free is not None:
                    self.part(c, token, self.hn_free)
                j, S, free = sq.take()
                a = act(lambda e: e.activation(S[:, 0:N], self.X[:, c, 0:N], ACT.Square), token, free)
                self.fed.append(token)
                if self.n == 0:
                    self.sum = dve(lambda e: e.tensor_copy(self.acc, S[:, 0:N]), a)
                else:
                    self.sum = dve(lambda e: e.tensor_tensor(self.acc, self.acc, S[:, 0:N], ALU.add), a, self.sum)
                sq.free[j] = [self.sum]
                self.n += 1

            def feed_all(self, token):
                end_late()
                for c in range(KC):
                    self.feed(c, token)

            def total(self):
                N = self.N
                p = pe(lambda e: e.matmul(PS[7][:, 0:N], ONES, self.acc, start=True, stop=True),
                       self.sum, t_const, bank_free[7])
                a = act(lambda e: e.activation(self.acc, PS[7][:, 0:N], ACT.Ln, bias=EPSC[:, 0:1], scale=1.0 / D),
                        p, t_eps)
                bank_free[7] = [a]
                self.r = act(lambda e: e.activation(self.acc, self.acc, ACT.Exp, scale=-0.5), a)

            def finish(self, hn_free):
                if not self.out:
                    for c in range(KC):
                        self.part(c, self.fed[c], hn_free)

            def normed(self, name, layer, col):
                b, p = dense(name, layer, col, self.out, self.N)
                if self.r is None:
                    self.total()
                out = PS[b][:, 0:self.N]
                return b, dve(lambda e: e.tensor_tensor(out, out, self.acc, ALU.mult), p, self.r), p

        def square_sums(S, r, N, ones, a, end):
            w, (SQH, SQL), free = sq_parts.take()
            t = split(S[r, 0:N], SQH[r, 0:N], SQL[r, 0:N], a, free)

            def sums(j, scale):
                b = aux_bank()
                pe(lambda e: e.matmul(PS[b][:, 0:N], ones[r, :], SQH[r, 0:N], start=True, stop=False), t, t_cr,
                   bank_free[b], signal=False)
                p = pe(lambda e: e.matmul(PS[b][:, 0:N], ones[r, :], SQL[r, 0:N], start=False, stop=True))
                sq_parts.free[w] = [p]
                soon.append(lambda: root(p, b, j, scale))

            def root(p, b, j, scale):
                i, R, free = rs.take()
                x = act(lambda e: e.activation(S[r, 0:N], PS[b][r, 0:N], ACT.Identity, bias=EPSC[r, 0:1], scale=scale),
                        p, t, a, t_eps)
                bank_free[b] = [x]
                y = act(lambda e: e.activation(R[r, 0:N], S[r, 0:N], ACT.Ln), x, free)
                y = act(lambda e: e.activation(R[r, 0:N], R[r, 0:N], ACT.Exp, scale=-0.5), y)
                y = pool(lambda e: e.tensor_tensor(S[r, 0:N], S[r, 0:N], R[r, 0:N], ALU.mult), y)

                def newton():
                    z = dve(lambda e: e.scalar_tensor_tensor(S[r, 0:N], S[r, 0:N], -0.5, R[r, 0:N], ALU.mult,
                                                             ALU.mult), y)
                    z = dve(lambda e: e.scalar_tensor_tensor(R[r, 0:N], S[r, 0:N], 1.5, R[r, 0:N], ALU.add,
                                                             ALU.mult), z)
                    sq.free[j] = [z]
                    return z
                late.append(lambda: end(i, R, newton(), x))
            return sums

        def head_norm(bank, done, N, scale, outs, res):
            r = slice(0, 128)
            j, S, free = sq.take()
            a = act(lambda e: e.activation(S[:, 0:N], PS[bank][:, 0:N], ACT.Square), done, free)

            def end(i, R, y, a):
                for rows, gain, dst in outs:
                    g = dve(lambda e, r=rows, g=gain, d=dst: e.scalar_tensor_tensor(
                        d, PS[bank][r, 0:N], par(g, 0, r), R[r, 0:N], ALU.mult, ALU.mult), y, a, done, t_gain)
                rs.free[i] = [g]
                bank_free[bank] = [a, g]
                res.append(g)

            sums = square_sums(S, r, N, BLKR, a, end)
            yield
            sums(j, scale)

        def to_rows(bank, done, N, put, res):
            i, B, free = tmp.take()
            a = act(lambda e: e.activation(B[:, 0:N], PS[bank][:, 0:N], ACT.Copy), done, free)
            bank_free[bank] = [a]
            yield
            b = aux_bank()
            for k in range(N // 128):
                p = pe(lambda e, k=k: e.transpose(PS[b][:, 128 * k:128 * k + 128], B[:, 128 * k:128 * k + 128], IDENT),
                       a, t_const, bank_free[b] if k == 0 else [], signal=(k == N // 128 - 1))
            tmp.free[i] = [p]
            t = dve(lambda e: put(e, PS[b][:, 0:N].rearrange("p (k f) -> p k f", f=128)), p)
            bank_free[b] = [t]
            res.append(t)

        def rope(src, got, which, rot, adds, res):
            b = aux_bank()
            p = pe(lambda e: e.matmul(PS[b][:, :], rot, src, start=True, stop=True), got, t_const, bank_free[b])
            i, A, fa = tmp.take()
            k, B, fb = tmp.take()
            x = dve(lambda e: e.tensor_tensor(A[:, :], src, ROPE[:, 2 * which, :], ALU.mult), got, fa, t_rope)
            y = dve(lambda e: e.tensor_tensor(B[:, :], PS[b][:, :], ROPE[:, 2 * which + 1, :], ALU.mult), p, fb, t_rope)
            bank_free[b] = [y]
            for rows, dst in adds:
                z = dve(lambda e, r=rows, d=dst: e.tensor_tensor(d, A[r, :], B[r, :], ALU.add), x, y)
                res.append(z)
            tmp.free[i] = tmp.free[k] = [z]
            return p

        class Job:
            def __init__(self, q, k, v, tiles, chunk, half, got, sink=None, loaded=None):
                self.q, self.k, self.v, self.tiles = q, k, v, tiles
                self.chunk, self.half, self.got, self.sink, self.loaded = chunk, half, got, sink, loaded

        def attention(jobs, got_hn):
            ring = {"s": 0, "t": 0}
            flat = [(n, i) for n, job in enumerate(jobs) for i in range(4)]
            live = {}
            result = []

            def load(n):
                job = jobs[n]
                w, (qh, ql, kh, kl), free = parts_of.take()
                c = {"slot": w, "rows": job.q[1], "got": []}
                r = job.q[1]
                nk = job.k.shape[1]
                c["q"], c["k"] = (qh[r, :], ql[r, :]), (kh[r, 0:nk], kl[r, 0:nk])
                for src, (h, l) in ((job.q[0], c["q"]), (job.k, c["k"])):
                    a = act(lambda e, h=h, src=src: e.activation(h, src, ACT.Copy), job.got, free)
                    b = pool(lambda e, h=h, l=l, src=src: e.tensor_tensor(l, src, h, ALU.subtract), a, job.got, free)
                    c["got"] += [a, b]
                if job.loaded is not None:
                    job.loaded(c["got"])
                j, St, free = stats.take()
                c["stat"], c["St"], c["stat_free"] = j, St, free
                live[n] = c

            def score(n, i):
                job, c = jobs[n], live[n]
                k0, nk, masks = job.tiles[i]
                b = ring["s"] % 3
                ring["s"] += 1
                pe.wait(bank_free[b], c["got"], t_cb)
                q, k = c["q"], c["k"]
                for x, (u, v) in enumerate(((0, 0), (0, 1), (1, 0))):
                    p = pe(lambda e, u=u, v=v, x=x: e.matmul(
                        PS[b][:, 0:nk], q[u][:, 128 * i:128 * i + 128], k[v][:, k0:k0 + nk], start=(x == 0),
                        stop=(x == 2 and not masks)), signal=(x == 2 and not masks))
                for m, (col, mask) in enumerate(masks):
                    last = m == len(masks) - 1
                    p = pe(lambda e, col=col, mask=mask, last=last: e.matmul(
                        PS[b][:, col:col + 128], IDB, mask, start=False, stop=last), signal=last)
                if i == 3:
                    parts_of.free[c["slot"]] = [p]
                St = c["St"]
                m = dve(lambda e: e.tensor_reduce(St[:, 0, i:i + 1], PS[b][:, 0:nk], AX, ALU.max, negate=True),
                        p, c["stat_free"])
                if job.sink is not None:
                    m = dve(lambda e: e.tensor_tensor(St[:, 0, i:i + 1], St[:, 0, i:i + 1],
                                                      NSINK[:, job.sink:job.sink + 1], ALU.min), m, t_gain)
                return b, m, p

            def powers(n, i, b, m, p):
                c = live[n]
                nk, St = jobs[n].tiles[i][1], c["St"]
                j, P, free = pp.take()
                a = act(lambda e: e.activation(P[:, 0:nk], PS[b][:, 0:nk], ACT.Exp, bias=St[:, 0, i:i + 1],
                                               accum_out=St[:, 1, i:i + 1]), m, p, free, c["stat_free"])
                bank_free[b] = [a]
                return j, P, a

            def turn(n, i, j, P, a):
                k0, nk, _ = jobs[n].tiles[i]
                b = 3 + ring["t"] % 2
                ring["t"] += 1
                pe.wait(bank_free[b], a)
                for k in range(nk // 128):
                    p = pe(lambda e, k=k: e.transpose(PS[b][:, 128 * k:128 * k + 128], P[:, 128 * k:128 * k + 128],
                                                      IDENT), signal=(k == nk // 128 - 1))
                pp.free[j] = [p]
                m, H, free = pt.take()
                t = dve(lambda e: e.tensor_copy(H[:, 0:nk], PS[b][:, 0:nk]), p, free)
                bank_free[b] = [t]
                return m, H, t

            def values(n, i, m, H, t):
                job, c = jobs[n], live[n]
                k0, nk, _ = job.tiles[i]
                b = 6 + n % 2
                pe.wait(t, job.got, bank_free[b] if i == 0 else [])
                nb = nk // 128
                for k in range(nb):
                    p = pe(lambda e, k=k: e.matmul(
                        PS[b][:, 64 * i:64 * i + 64], H[:, 128 * k:128 * k + 128], job.v[:, k0 // 128 + k, :],
                        start=(k == 0), stop=(k == nb - 1)), signal=(k == nb - 1))
                pt.free[m] = [p]
                return p

            def finish(n, p, a):
                job, c = jobs[n], live.pop(n)
                St = c["St"]
                if job.sink is not None:
                    x = act(lambda e: e.activation(St[:, 2, :], St[:, 0, :], ACT.Exp, bias=par("sink", job.sink)),
                            t_par, a)
                    a = [a, dve(lambda e: e.tensor_tensor(St[:, 1, :], St[:, 1, :], St[:, 2, :], ALU.add), x, a)]
                r = dve(lambda e: e.reciprocal(St[:, 3, :], St[:, 1, :]), a)
                if job.half == 0:
                    live["o"] = ot.take()
                j, O, free = live["o"]
                b, f = 6 + n % 2, 64 * job.half
                t = dve(lambda e: e.tensor_tensor(
                    O[:, :, f:f + 64], PS[b][:, 0:256].rearrange("p (i d) -> p i d", d=64),
                    St[:, 3, :].unsqueeze(2).broadcast_to([128, 4, 64]), ALU.mult), r, p, free)
                bank_free[b] = [t]
                stats.free[c["stat"]] = [t]
                if job.half == 1:
                    start(spread(job.chunk, j, O, t))

            def spread(chunk, j, O, t):
                yield
                for i in range(4):
                    p = pe(lambda e, i=i: e.transpose(PS[5][:, 128 * i:128 * i + 128], O[:, i, :], IDENT),
                           t, bank_free[5] if i == 0 else [], signal=(i == 3))
                ot.free[j] = [p]
                bank_free[5] = split(PS[5][:, :], HNh[:, chunk, :], HNl[:, chunk, :], p, got_hn)
                result.extend(bank_free[5])

            A, B = {}, {}
            ot.free[0], ot.free[1] = tmp.free[0], tmp.free[1]
            load(0)
            for s in range(len(flat) + 4):
                if 0 <= s - 3 < len(flat):
                    n2, i2 = flat[s - 3]
                    B[s - 3] = turn(n2, i2, *A[s - 3])
                if s < len(flat):
                    n, i = flat[s]
                    S = score(n, i)
                if s < len(flat):
                    A[s] = powers(n, i, *S)
                if 0 <= s - 4 < len(flat):
                    n3, i3 = flat[s - 4]
                    p = values(n3, i3, *B[s - 4])
                    if i3 == 3:
                        finish(n3, p, A[s - 4][2])
                if s < len(flat) and i == 0 and n + 1 < len(jobs):
                    load(n + 1)
                tick()
            flush()
            tmp.free[0], tmp.free[1] = ot.free[0], ot.free[1]
            return result

        def spill():
            n = spilled[0] = spilled[0] + 1
            pool_q(lambda e: e.dma_start(io["spill"], XT[:, :, :]).then_inc(s_spill, 16), norm.fed, signal=False)
            return [(s_spill, 16 * n), norm.sum] + [t for _, _, got in norm.out for t in got]

        def refill(n_fill):
            def go_on(got):
                pool_q(lambda e: e.dma_start(XT[:, :, :], io["spill"]).then_inc(s_fill, 16), got, [t_spill],
                       signal=False)
            return go_on

        spilled = [0]

        def project(name, layer, got, norm, filled=None):
            rhs = [(HNh[:, c, :], HNl[:, c, :], got) for c in range(KC)]
            for c in range(KC):
                b, p = dense(name, layer, 128 * c, rhs)
                t = dve(lambda e, b=b, c=c: e.tensor_tensor(XT[:, c, :], PS[b][:, :], XT[:, c, :], ALU.add), p, filled)
                bank_free[b] = [t]
                norm.feed(c, t)
                tick()
            return p

        def ffn(gate, up, down, layer, off, last, conv, weight, norm):
            g_free = [None]
            for s in range(2):
                parts = [None] * HALF

                def conv_part(b, p, idx, lay, box):
                    k, B, free = cv.take()
                    w = lambda tap: par(f"cw{lay}", 3 * idx + tap)
                    a = act(lambda e: e.activation(B[:, :], PS[b][:, :], ACT.Identity, bias=par(f"cb{lay}", idx),
                                                   scale=w(2)), p, free, t_par)
                    a = dve(lambda e: e.scalar_tensor_tensor(B[:, 1:T], PS[b][:, 0:T - 1], w(1), B[:, 1:T],
                                                             ALU.mult, ALU.add), a, p)
                    a = dve(lambda e: e.scalar_tensor_tensor(B[:, 2:T], PS[b][:, 0:T - 2], w(0), B[:, 2:T],
                                                             ALU.mult, ALU.add), a)
                    bank_free[b] = [a]
                    box.append((k, B, a))

                for q in range(HALF):
                    c = HALF * s + q
                    if conv:
                        box = []
                        for idx in (c, FC + c):
                            b, p, hn_done = last.normed(gate, layer, 128 * idx)
                            conv_part(b, p, idx, layer, box)
                            tick()
                        (k0, A, ta), (k1, B, tb) = box
                        a = act(lambda e, A=A: e.activation(A[:, :], A[:, :], ACT.Silu), ta)
                        i, G, free = gf.take()
                        t = dve(lambda e, G=G, A=A, B=B: e.tensor_tensor(G[:, :], A[:, :], B[:, :], ALU.mult), a, tb, free)
                        cv.free[k0] = cv.free[k1] = [t]
                    else:
                        b, p, _ = last.normed(gate, layer, 128 * c)
                        k0, A, free = cv.take()
                        a = act(lambda e, A=A, b=b: e.activation(A[:, :], PS[b][:, :], ACT.Silu), p, free)
                        bank_free[b] = [a]
                        tick()
                        b, p, hn_done = last.normed(up, layer, 128 * c)
                        i, G, free = gf.take()
                        t = dve(lambda e, G=G, A=A, b=b: e.tensor_tensor(G[:, :], A[:, :], PS[b][:, :], ALU.mult),
                                a, p, free)
                        cv.free[k0] = [t]
                        bank_free[b] = [t]
                        tick()
                    h, l = Gh[:, q, :], Gl[:, q, :]
                    w = split(G[:, :], h, l, t, g_free[0])
                    gf.free[i] = w
                    parts[q] = (h, l, w)
                if s == 1 and norm is not None:
                    norm.hn_free = [hn_done]
                for c in range(KC):
                    b, p = dense(down, layer, 128 * c, parts, row0=128 * HALF * s)
                    t = dve(lambda e, b=b, c=c: e.scalar_tensor_tensor(XT[:, c, :], PS[b][:, :], weight, XT[:, c, :],
                                                                       ALU.mult, ALU.add), p)
                    bank_free[b] = [t]
                    if s == 1:
                        if norm is not None:
                            norm.feed(c, t)
                        else:
                            dma(io["out"][:, c, :], XT[:, c, :], s_out, 16 * (c + 1), t)
                    tick()
                g_free[0] = p
            return p

        t_par = dma(PAR[:, :], io["par"], s_par, 16)
        t_const = dma(CONST[:, :], io["const"], s_const, 16)
        C0 = VA[:, 0, 0:640]
        t_x = dma(XT[:, :, :], io["x"], s_x, 16)
        t_c0 = dma(C0, io["cr"], s_cr, 16)
        W.load_to(NRAW - 1)
        MT = [MT0, MT1]
        t_mem = []
        for m in range(2):
            t_mem.append(dma(MT[m][:, :, :], io["mem"][m], s_mem, 16 * (m + 1), t_mem))
        t_cb = dma(CB[:, :], io["cb"], s_cb, 16)

        t_cr = act(lambda e: e.activation(CR[:, :], C0, ACT.Copy), t_c0)
        t_eps = pool(lambda e: e.memset(EPSC[:, 0:1], EPS))
        t_one = pool(lambda e: e.memset(EPSC[:, 1:2], 1.0))
        pool(lambda e: e.tensor_scalar(NSINK[:, :], par("sink", 0, n=8), -1.0, None, ALU.mult), t_par)
        t_gain = pool(lambda e: e.tensor_scalar(par("mq0", 0, n=5), par("mq0", 0, n=5), 0.125, None, ALU.mult), t_par)
        t_gain = pool(lambda e: e.tensor_scalar(par("mlaq"), par("mlaq"), 96.0 ** -0.5, None, ALU.mult), t_gain)
        act(lambda e: e.preload_act_table_set(TABLES), signal=False)

        def memories(p_in, norms):
            for nm in norms:
                nm.finish([p_in])
            for m in range(2):
                for c in range(4):
                    b, p, pp_ = norms[m].normed(("w_mem_kv", "w_mem_kv_2")[m], 0, 128 * c)
                    tick()
                    if c < 2:
                        dst = [(0, "mk0"), (1, "mk1")] if m == 0 else [(2, "gmk2")]
                        go(head_norm(b, p, MEM, 1 / 64, [(slice(0, 128), gn, KMEM[:, x, c, :]) for x, gn in dst],
                                     kv_got[m]))
                    else:
                        go(to_rows(b, p, MEM, lambda e, s, m=m, c=c: e.tensor_copy(
                            VMEM[:, m, :, 128 * (c - 2):128 * (c - 1)], s), kv_got[m]))
            return pp_

        kv_got = [[], []]
        norm = ColumnNorm(XT, "mix0", hn_free=[])
        norm.feed_all(t_x)

        def mem_jobs(m, km):
            return [Job((MQ[rows, c, :], rows), KMEM[rows, km, c, :], VMEM[:, m, :, 64 * (2 * c + x):64 * (2 * c + x) + 64],
                        [(0, MEM, [])] * 4, 6 + c, x, [mix_got, kv_got[m]])
                    for c in range(2) for x, rows in ((0, lo), (1, hi))]

        lo, hi = slice(0, 64), slice(64, 128)

        def go(g):
            try:
                next(g)
                start(g)
            except StopIteration:
                pass

        mix_got = []
        t_rope = []
        CUM, NCUM = (VA[0:12, k, 0:T] for k in range(2))
        t_spill = spill()
        tq = pool(lambda e: e.memset(QA[64:66, :, :], 1.0))
        pool(lambda e: e.memset(XT[64:66, :, :], 1.0), t_spill)
        tk = pool(lambda e: e.memset(KB[64:66, :, :], 1.0))

        def decay(b, p):
            f, A, fa = tmp.take()
            k, B, fb = tmp.take()
            j, C, fc = sq.take()
            r = slice(0, 12)
            z = dve(lambda e: e.tensor_scalar(A[r, :], PS[b][r, :], par("bf", 0, r), None, ALU.add), p, fa, t_par)
            bank_free[b] = [z]
            x = act(lambda e: e.activation(B[r, :], A[r, :], ACT.Abs), z, fb)
            y = act(lambda e: e.activation(B[r, :], B[r, :], ACT.Exp, scale=-1.0), x)
            y = act(lambda e: e.activation(B[r, :], B[r, :], ACT.Ln, bias=EPSC[r, 1:2]), y, t_one)
            o = dve(lambda e: e.memset(C[r, :], 1.0), fc)
            z = dve(lambda e: e.tensor_scalar(A[r, :], A[r, :], 0.0, None, ALU.min), z, x)
            z = dve(lambda e: e.tensor_tensor(A[r, :], A[r, :], B[r, :], ALU.subtract), z, y)
            z = dve(lambda e: e.tensor_tensor_scan(CUM, C[r, :], A[r, :], 0.0, ALU.mult, ALU.add), z, o, t_cr)
            w = dve(lambda e: e.tensor_scalar(NCUM, CUM, -1.0, None, ALU.mult), z)
            tmp.free[f] = tmp.free[k] = [z]
            sq.free[j] = [z]
            mix_got.append(dma(QA[65:66, :, :], CUM, s_cum, 16, z, tq))
            mix_got.append(dma(XT[64:65, :, :], NCUM[0:8], s_cum, 32, w, tk, mix_got[-1]))
            mix_got.append(dma(KB[64:65, :, :], NCUM[8:12], s_cum, 48, w, tk, mix_got[-1]))

        mem_norms = [ColumnNorm(MT[m], ("memn", "memn2")[m], MEM, MEM * m, ACCM[:, m, :]) for m in range(2)]
        for n, c in enumerate(range(21)):
            b, p, done = norm.normed("fox", 0, 128 * c)
            tick()
            if c == 8:
                mem_norms[0].feed_all(t_mem[0])
            if c == 14:
                mem_norms[1].feed_all(t_mem[1])
            if c == 0:
                decay(b, p)
            elif c < 13:
                g, ch = ("foxq", c - 1) if c < 7 else ("foxk", c - 7)
                d = [QA[lo, 2 * ch + x, :] if c < 7 else key_rows(lo, 2 * ch + x) for x in range(2)]
                go(head_norm(b, p, T, 1 / 64, [(lo, g, d[0]), (hi, g, d[1])], mix_got))
            elif c < 19:
                ch = c - 13
                dve.wait((s_cum, 48))
                go(to_rows(b, p, T, lambda e, s, ch=ch: e.tensor_copy(VA[:, :, 128 * ch:128 * ch + 128], s), mix_got))
            else:
                go(head_norm(b, p, T, 1 / 64, [(slice(0, 128), "mq0", MQ[:, c - 19, :])], mix_got))
        p = memories(done, mem_norms)
        flush()

        def full_jobs(rows, m, km):
            tiles = [(0, 128 * (i + 1), [(128 * i, MCAUS)]) for i in range(4)]
            return [Job((QA[rows, h, :], rows), key_rows(rows, h), VA[:, :, 64 * h:64 * h + 64], tiles, h // 2, h % 2,
                        mix_got, loaded=refill(m) if h == 7 else None) for h in range(12)] + mem_jobs(m, km)

        got = attention(full_jobs(slice(0, 66), 0, 0), [p])
        norm = ColumnNorm(XT, "nf0")
        p = project("w_out", 0, got, norm, (s_fill, 16))
        norm.finish([p])
        last, norm = norm, ColumnNorm(XT, "mix1")
        p = ffn("ffn_w_up", "ffn_w_up", "ffn_w_down", 0, FF, last, True, 1.0, norm)
        act(lambda e: e.preload_act_table_set(TABLES), signal=False)

        mix_got = []
        t_rope.clear()

        def tables():
            i, PF, free = tmp.take()
            t_pos = []
            for m in range(2):
                pool(lambda e, m=m: e.dma_start(POS[m], io["pos"][m]).then_inc(s_pos, 16), p, signal=False)
                t_pos.append((s_pos, 16 * (m + 1)))
            A, N, NF = (VA[:, k, 0:T] for k in (1, 2, 3))
            NI = N.bitcast(I32)
            last = []
            for w in range(2):
                z = dve(lambda e, w=w: e.tensor_copy(PF[:, :], POS[w]), t_pos, free, last)
                a = dve(lambda e, w=w: e.tensor_scalar(A, PF[:, :], par(f"fr{w}"), None, ALU.mult), z, t_par, last)
                for k, quarter in ((0, 0.25), (1, 0.0)):
                    x = dve(lambda e, q=quarter: e.tensor_scalar(NI, A, 1 / (2 * PI), q, ALU.mult, ALU.add), a, last)
                    x = dve(lambda e: e.tensor_copy(NF, NI), x)
                    R = ROPE[:, 2 * w + k, :]
                    x = dve(lambda e, R=R: e.scalar_tensor_tensor(R, NF, -C1, A, ALU.mult, ALU.add), x)
                    x = dve(lambda e, R=R: e.scalar_tensor_tensor(R, NF, -C2, R, ALU.mult, ALU.add), x)
                    x = dve(lambda e, R=R: e.scalar_tensor_tensor(R, NF, -C3, R, ALU.mult, ALU.add), x)
                    x = dve(lambda e, R=R, q=quarter: e.tensor_scalar(R, R, 2 * PI * q, PI, ALU.add, ALU.min), x)
                    x = dve(lambda e, R=R: e.tensor_scalar(R, R, -PI, None, ALU.max), x)
                    last = [x]
                    t_rope.append(x)
            tmp.free[i] = last
            x = None
            for k in range(4):
                R = ROPE[:, k, :]
                x = act(lambda e, R=R: e.activation(R, R, ACT.Sin), t_rope[k])
            t_rope[:] = [x]
            act(lambda e: e.preload_act_table_set(TABLES), signal=False)
            return last

        t_spill = spill()
        POS = [VA[:, 0, 0:T].bitcast(I32), MQ[:, 0, :].bitcast(I32)]
        t_va = tables()
        lat, krd = [], []
        banks = []
        for c in range(6):
            b, p, p_in = norm.normed("mla", 0, 128 * c)
            tick()
            banks.append((b, p))
            if c == 2:
                i, KR, free = tmp.take()
                a = act(lambda e, b=b: e.activation(KR[:, :], PS[b][:, :], ACT.Copy), p, free)
                bank_free[b] = [a]
            if c < 2:
                go(head_norm(b, p, T, 1 / 64, [(slice(0, 128), "mq1", MQ[:, c, :])], mix_got))
        flush()
        kr = []
        KRR = pp.items[2][:, :]
        p_rot = rope(KR[:, :], a, 0, PM, [(slice(0, 128), KRR)], kr)
        tmp.free[i] = [p_rot, kr[-1]]
        pool(lambda e: e.tensor_copy(XT[64:96, :, :], KRR[64:96].unsqueeze(1).broadcast_to([32, 8, T])), kr, t_spill)
        tk = pool(lambda e: e.tensor_copy(KB[64:96, :, :], KRR[64:96].unsqueeze(1).broadcast_to([32, 4, T])), kr)
        def latent_norm(chunks, gain, scale):
            bb = aux_bank()
            for n, c in enumerate(chunks):
                b, pc = banks[3 + c]
                j, S, free = sq.take()
                a = act(lambda e, b=b, S=S: e.activation(S[:, :], PS[b][:, :], ACT.Square), pc, free)
                p = pe(lambda e, n=n, S=S: e.matmul(PS[bb][:, :], ONES, S[:, :], start=(n == 0),
                                                    stop=(n == len(chunks) - 1)), a, bank_free[bb] if n == 0 else [])
                sq.free[j] = [p]
            i, R, a = rsqrt(bb, slice(0, 128), T, scale, p)
            for n, c in enumerate(chunks):
                b, pc = banks[3 + c]
                k, B, free = tmp.take()
                g = dve(lambda e, b=b, B=B, n=n: e.scalar_tensor_tensor(B[:, :], PS[b][:, :], par(gain, n), R[:, :],
                                                                        ALU.mult, ALU.mult), a, pc, free)
                bank_free[b] = [g]
                t = split(B[:, :], HNh[:, c, :], HNl[:, c, :], g, p_in)
                tmp.free[k] = t
                lat.append((HNh[:, c, :], HNl[:, c, :], t))
            rs.free[i] = [g]

        latent_norm((0, 1), "qa", 1 / 256)
        latent_norm((2,), "kva", 1 / 128)

        def query_rows(r, h):
            return QA[r, h, :]

        q_raw = [[] for _ in range(12)]
        k_raw = [[tk] for _ in range(12)]

        def copies(b, p, A, c, raw):
            x = act(lambda e: e.activation(A(lo, 2 * c), PS[b][0:64, :], ACT.Copy), p, t_spill)
            y = dve(lambda e: e.tensor_copy(A(lo, 2 * c + 1), PS[b][64:128, :]), p, t_spill)
            raw[2 * c].append(x)
            raw[2 * c + 1].append(y)
            bank_free[b] = [x, y]

        def rope_chunk(b, p, r):
            i, B, free = tmp.take()
            a = act(lambda e: e.activation(B[:, :], PS[b][:, :], ACT.Copy), p, free)
            bank_free[b] = [a]
            yield
            res = []
            x = rope(B[:, :], a, 0, PM, [(slice(32 * j, 32 * j + 32), QA[64:96, 4 * r + j, :]) for j in range(4)], res)
            tmp.free[i] = [x, res[-1]]
            for j in range(4):
                q_raw[4 * r + j].append(res[j])

        summed = [0, None]

        def sum96(A, h, raw):
            r = slice(0, 96)
            j, S, free = sq.take()
            row = summed[0]
            summed[0] += 1
            if A is key_rows:
                a = pool(lambda e: e.tensor_tensor(S[r, :], A(r, h), A(r, h), ALU.mult), raw, free)
            else:
                a = act(lambda e: e.activation(S[r, :], A(r, h), ACT.Square), raw, free)
            w, (SQH, SQL), free = sq_parts.take()
            t = split(S[r, :], SQH[r, :], SQL[r, :], a, free)
            sq.free[j] = t
            yield
            pe(lambda e: e.matmul(PS[7][:, :], to_row(row)[r, :], SQH[r, :], start=(row == 0), stop=False), t, t_cr,
               bank_free[7] if row == 0 else [], signal=False)
            summed[1] = pe(lambda e: e.matmul(PS[7][:, :], to_row(row)[r, :], SQL[r, :], start=False,
                                              stop=(row == 23)))
            sq_parts.free[w] = [summed[1]]

        def scale96():
            r = slice(0, 24)
            j, S, free = sq.take()
            i, R, free2 = rs.take()
            w, (RH, RL), free3 = sq_parts.take()
            x = dve(lambda e: e.tensor_scalar(S[r, :], PS[7][r, :], 1 / 96, EPS, ALU.mult, ALU.add), summed[1], free)
            bank_free[7] = [x]
            y = act(lambda e: e.activation(R[r, :], S[r, :], ACT.Ln), x, free2)
            y = act(lambda e: e.activation(R[r, :], R[r, :], ACT.Exp, scale=-0.5), y)
            z = dve(lambda e: e.tensor_tensor(S[r, :], S[r, :], R[r, :], ALU.mult), y)
            z = dve(lambda e: e.scalar_tensor_tensor(S[r, :], S[r, :], -0.5, R[r, :], ALU.mult, ALU.mult), z)
            z = dve(lambda e: e.scalar_tensor_tensor(R[r, :], S[r, :], 1.5, R[r, :], ALU.add, ALU.mult), z)
            t = split(R[r, :], RH[r, :], RL[r, :], z, free3)
            sq.free[j] = rs.free[i] = t
            r96 = slice(0, 96)
            for row in range(24):
                A, h, gain, raw = (key_rows, row, "mlak", k_raw) if row < 12 else (query_rows, row - 12, "mlaq", q_raw)
                b = (5, 6, 3, 4)[row % 4]
                lhs = IDENTR[r, row:row + 1].broadcast_to([24, 128])
                pe(lambda e, b=b, lhs=lhs: e.matmul(PS[b][:, :], lhs, RH[r, :], start=True, stop=False), t,
                   bank_free[b], signal=False)
                p = pe(lambda e, b=b, lhs=lhs: e.matmul(PS[b][:, :], lhs, RL[r, :], start=False, stop=True))
                g = dve(lambda e, A=A, h=h, gain=gain, b=b: e.scalar_tensor_tensor(
                    A(r96, h), A(r96, h), par(gain, 0, r96), PS[b][r96, :], ALU.mult, ALU.mult),
                    p, raw[h], t_gain)
                bank_free[b] = [g]
            sq_parts.free[w] = [p]
            mix_got.append(g)

        for c in range(9):
            b, p = dense("mla_q", 0, 128 * c, lat[0:2])
            tick()
            if c < 6:
                copies(b, p, query_rows, c, q_raw)
            else:
                go(rope_chunk(b, p, c - 6))
        flush()
        for c in range(12):
            b, p = dense("mla_kv", 0, 128 * c, lat[2:3])
            tick()
            if c < 6:
                copies(b, p, key_rows, c, k_raw)
                go(sum96(key_rows, 2 * c, k_raw[2 * c]))
                go(sum96(key_rows, 2 * c + 1, k_raw[2 * c + 1]))
            else:
                ch = c - 6
                go(to_rows(b, p, T, lambda e, s, ch=ch: e.tensor_copy(VA[:, :, 128 * ch:128 * ch + 128], s), mix_got))
                go(sum96(query_rows, 2 * ch, q_raw[2 * ch]))
                go(sum96(query_rows, 2 * ch + 1, q_raw[2 * ch + 1]))
        flush()
        scale96()
        got = attention(full_jobs(slice(0, 96), 0, 1), [p])
        norm = ColumnNorm(XT, "nf1")
        p = project("w_out", 1, got, norm, (s_fill, 32))
        norm.finish([p])
        last, norm = norm, ColumnNorm(XT, "f1")
        p = ffn("ffn_w_up", "ffn_w_up", "ffn_w_down", 1, FF, last, True, 1.0, norm)
        act(lambda e: e.preload_act_table_set(TABLES), signal=False)

        last, norm = norm, ColumnNorm(XT, "mix2")
        p = ffn("w_ffn1_gate_2", "w_ffn1_up_2", "w_ffn1_down_2", 0, 0, last, False, 0.5, norm)
        act(lambda e: e.preload_act_table_set(TABLES), signal=False)

        mix_got = []
        HP = QA[:, 5:8, :].rearrange("p h t -> p (h t)")
        HW = T + 30
        HX = [HP[:, 0:HW], HP[:, HW:2 * HW]]
        CA = [QA[:, 8, :], QA[:, 9, :]]
        SG = [QA[:, 10, :], QA[:, 11, :]]
        zero = [pool(lambda e, c=c: e.memset(HX[c][:, 0:30], 0.0), p) for c in range(2)]
        q_rot = [[] for _ in range(5)]

        def rotated(n):
            res = []
            yield
            yield
            rope(QA[:, n, :], q_rot[n], 1, PB, [(slice(0, 128), QA[:, n, :])], res)
            mix_got.extend(res)

        glu = {}

        conv_done = []
        attending = [True]

        def conformer():
            t = [None, None]
            for n in range(2):
                t[n] = dve(lambda e, n=n: e.tensor_scalar(CA[n], HX[n][:, 30:30 + T], par("dw", 31 * n + 30),
                                                          par("db", n), ALU.mult, ALU.add), glu[n])
                for k in range(30):
                    if k % 2 == 0:
                        yield
                    t[n] = dve(lambda e, n=n, k=k: e.scalar_tensor_tensor(CA[n], HX[n][:, k:k + T], par("dw", 31 * n + k),
                                                                          CA[n], ALU.mult, ALU.add), t[n])
            while attending[0]:
                yield
            b = 5
            for n in range(2):
                p = pe(lambda e, n=n: e.matmul(PS[b][:, :], ONES, CA[n], start=(n == 0), stop=(n == 1)), t,
                       bank_free[b] if n == 0 else [])
            for n in range(2):
                t[n] = dve(lambda e, n=n: e.scalar_tensor_tensor(CA[n], PS[b][:, :], -1 / 256, CA[n], ALU.mult,
                                                                 ALU.add), p, t[n])
            bank_free[b] = [t[1]]
            a = []
            for n in range(2):
                a.append(act(lambda e, n=n: e.activation(SG[n], CA[n], ACT.Square), t[n]))
            for n in range(2):
                p = pe(lambda e, n=n: e.matmul(PS[b][:, :], ONES, SG[n], start=(n == 0), stop=(n == 1)), a,
                       bank_free[b] if n == 0 else [])
            j, R, x = rsqrt(b, slice(0, 128), T, 1 / 256, p)
            for n in range(2):
                t[n] = dve(lambda e, n=n: e.scalar_tensor_tensor(CA[n], CA[n], par("lg", n), R[:, :], ALU.mult,
                                                                 ALU.mult), x, t[n])
            rs.free[j] = [t[1]]
            conv_done.extend(t)

        for c in range(12):
            b, p, p_in = norm.normed("w_in_2", 0, 128 * c)
            tick()
            if c < 2:
                a = act(lambda e, b=b, c=c: e.activation(SG[c], PS[b][:, :], ACT.Sigmoid), p)
                bank_free[b] = [a]
                glu[c] = a
                if c == 1:
                    act(lambda e: e.preload_act_table_set(TABLES), signal=False)
            elif c < 4:
                n = c - 2
                t = dve(lambda e, b=b, n=n: e.tensor_tensor(HX[n][:, 30:30 + T], PS[b][:, :], SG[n], ALU.mult),
                        p, glu[n], zero)
                bank_free[b] = [t]
                glu[n] = t
                if n == 1:
                    slow.append(conformer())
            elif c < 9:
                n = c - 4
                go(head_norm(b, p, T, 1 / 64, [(slice(0, 128), "gq2" if n < 4 else "gk2", QA[:, n, :])], q_rot[n]))
                go(rotated(n))
            elif c == 9:
                go(to_rows(b, p, T, lambda e, s: e.tensor_copy(VA[:, :, 0:128], s), mix_got))
            else:
                go(head_norm(b, p, T, 1 / 64, [(slice(0, 128), "gmq2", MQ[:, c - 10, :])], mix_got))
        flush()

        tiles = [(0, 128, [(0, MCAUS)])] + [(128 * (i - 1), 256, [(0, MPREV), (128, MCAUS)]) for i in range(1, 4)]
        blk = []
        for h in range(8):
            r = lo if h < 4 else hi
            blk.append(Job((QA[r, h % 4, :], r), QA[r, 4, :], VA[:, :, 64 * (h // 4):64 * (h // 4) + 64], tiles,
                           h // 2, h % 2, mix_got, sink=h))
        blk += mem_jobs(1, 2)
        attending[0] = True
        got = attention(blk, [p_in])
        attending[0] = False
        while slow:
            tick()
        for n in range(2):
            a = act(lambda e, n=n: e.activation(SG[n], CA[n], ACT.Silu, bias=par("lb", n)), conv_done)
            got.extend(split(SG[n], HNh[:, 4 + n, :], HNl[:, 4 + n, :], a, p_in))
        act(lambda e: e.preload_act_table_set(TABLES), signal=False)
        norm = ColumnNorm(XT, "f2")
        p = project("w_out_2", 0, got, norm)
        norm.finish([p])
        ffn("w_ffn2_gate_2", "w_ffn2_up_2", "w_ffn2_down_2", 0, 0, norm, False, 0.5, None)
        sp.wait((s_out, 16 * KC))
        assert W.at == len(plan)

        block = ctx.enter_context(nc.Block())
        block.tensor(pe.play)
        block.vector(dve.play)
        block.scalar(act.play)
        block.gpsimd(pool_q.play)
        block.sync(sp.play)


def lay_out(x):
    f = {k: np.asarray(v) for k, v in x.items()}
    fox = f["fox_w_in"][0]
    pad = np.zeros((D, 116), fox.dtype)
    mla = f["mla_w_in"][0]
    kr = mla[:, 384:416]
    qu = f["mla_w_q_up"][0].reshape(256, 12, 96)
    kvu = f["mla_w_kv_up"][0].reshape(128, 12, 128)
    w2 = f["w_in_2"][0]
    q2 = w2[:, 0:512].reshape(D, 2, 4, 64).transpose(0, 2, 1, 3).reshape(D, 512)
    src = {
        "w_mem_kv": f["w_mem_kv"], "w_mem_kv_2": f["w_mem_kv_2"][0],
        "fox": np.concatenate([fox[:, 2304:2316], pad, fox[:, :2304], fox[:, 2316:]], 1),
        "mla": np.concatenate([mla[:, 416:], kr, kr, kr, kr, mla[:, :384]], 1),
        "mla_q": np.concatenate([qu[:, :, :64].reshape(256, 768), qu[:, :, 64:].reshape(256, 384)], 1),
        "mla_kv": np.concatenate([kvu[:, :, :64].reshape(128, 768), kvu[:, :, 64:].reshape(128, 768)], 1),
        "w_in_2": np.concatenate([w2[:, 1024:1280], w2[:, 768:1024], q2, w2[:, 512:768], w2[:, 1280:]], 1),
    }

    def tile(key):
        name, layer, r, c = key
        a = src[name] if name in src else f[name][layer]
        return a[r:r + 128, c:c + 128]

    plan = weight_plan()
    n = (len(plan) + UT - 1) // UT
    w = np.zeros((n, 128, 128 * UT), np.float32)
    for i, key in enumerate(plan):
        w[i // UT, :, 128 * (i % UT):128 * (i % UT) + 128] = tile(key)

    def cols(a):
        return a.reshape(-1, 128).T

    def twice(a):
        return np.concatenate([a, a]).reshape(128, 1)

    def rows(a):
        return np.concatenate([a, np.zeros(128 - a.size, a.dtype)]).reshape(128, 1)

    fr0 = (10000.0 ** (-np.arange(0, 32, 2) / 32)).astype(np.float32)
    fr1 = (500000.0 ** (-np.arange(8) / 8)).astype(np.float32)
    half = np.concatenate([fr1, fr1, np.zeros(48, np.float32)])
    p = {
        "mix0": cols(f["norm_mix"][0]), "mix1": cols(f["norm_mix"][1]), "nf0": cols(f["norm_ffn"][0]),
        "nf1": cols(f["norm_ffn"][1]), "memn": cols(f["mem_norm"]), "f1": cols(f["g_ffn1_2"][0]),
        "mix2": cols(f["g_mix_2"][0]), "memn2": cols(f["g_mem_2"][0]), "f2": cols(f["g_ffn2_2"][0]),
        "mq0": twice(f["mem_q_gain"][0]), "mq1": twice(f["mem_q_gain"][1]), "foxq": twice(f["fox_q_gain"][0]),
        "gq2": twice(f["g_q_2"][0]), "gmq2": twice(f["g_mq_2"][0]), "mlaq": rows(f["mla_q_gain"][0]),
        "mk0": twice(f["mem_k_gain"][0]), "mk1": twice(f["mem_k_gain"][1]), "foxk": twice(f["fox_k_gain"][0]),
        "gk2": twice(f["g_k_2"][0]), "gmk2": twice(f["g_mk_2"][0]), "mlak": rows(f["mla_k_gain"][0]),
        "qa": cols(f["mla_qa_norm"][0]), "kva": cols(f["mla_kva_norm"][0]), "bf": rows(f["fox_b_f"][0]),
        "db": cols(f["b_dw_2"][0]), "lg": cols(f["g_conv_ln_2"][0]), "lb": cols(f["b_conv_ln_2"][0]),
        "dw": f["w_dw_2"][0].reshape(31, 2, 128).transpose(2, 1, 0).reshape(128, 62),
        "sink": np.broadcast_to(f["sinks_2"][0], (128, 8)),
        "fr0": np.tile(fr0, 8).reshape(128, 1), "fr1": np.concatenate([half, half]).reshape(128, 1),
    }
    for i in range(2):
        p[f"cw{i}"] = f["ffn_conv_w"][i].reshape(3, 44, 128).transpose(2, 1, 0).reshape(128, 132)
        p[f"cb{i}"] = cols(f["ffn_conv_b"][i])
    parts = [p[name] for name, _ in PARAMS]

    def chunks(a):
        return a.T.reshape(8, 128, -1).transpose(1, 0, 2)

    eye = np.eye(128, dtype=np.float32)
    blk = np.kron(np.eye(2), np.ones((64, 64)))

    def rot(width, half):
        m = np.zeros((128, 128))
        for g in range(0, 128, width):
            for j in range(half):
                m[g + j + half, g + j] = -1.0
                m[g + j, g + j + half] = 1.0
        return m

    const = np.concatenate([eye, np.ones((128, 128)), rot(32, 16), rot(64, 8)], 1).astype(np.float32)
    col = np.zeros((128, 256))
    col[:, 127] = 1.0
    cr = np.concatenate([np.ones((128, 128)), blk, eye, col], 1).astype(np.float32)
    q, k = np.arange(128)[:, None], np.arange(128)[None, :]
    cb = np.concatenate([eye, np.where(k <= q, 0.0, NEG), np.where(k > q, 0.0, NEG)], 1).astype(mybir.dt.np(BF16))
    return {
        "w": w, "par": np.concatenate(parts, 1), "const": const, "cr": cr, "cb": cb,
        "x": chunks(f["x"][0]), "mem": np.stack([chunks(f["mem"][0]), chunks(f["mem_2"][0])]),
        "pos": np.stack([np.broadcast_to(f[k][0], (128, T)) for k in ("positions", "positions_2")]),
    }


def kernel(**inputs):
    import concourse.bacc as bacc
    from concourse.bass_utils import run_bass_kernel_spmd as run

    nc = bacc.Bacc("TRN2", target_bir_lowering=False, num_devices=1)
    laid = {k: np.ascontiguousarray(v) for k, v in lay_out(inputs).items()}
    io = {k: nc.dram_tensor(f"in_{k}", v.shape, mybir.dt.from_np(v.dtype), kind="ExternalInput").ap()
          for k, v in laid.items()}
    io["spill"] = nc.dram_tensor("spill", (128, KC, T), F32, kind="Internal").ap()
    io["out"] = nc.dram_tensor("out_x", (128, KC, T), F32, kind="ExternalOutput").ap()
    program(nc, io)
    r = run(nc, [{f"in_{k}": v for k, v in laid.items()}], core_ids=[0])
    got = r.results[0]["out_x"]
    return np.ascontiguousarray(got.transpose(1, 0, 2).reshape(D, T).T)[None]
```
